# Optimizing a Trainium2 kernel written in Bass

```python
import jax, jax.numpy as jnp
from jax import lax
import numpy as np
import math

D_MODEL = 1024
BATCH = 1
SEQ = 256
DEPTH = 2

RNN_WIDTH = 1024
RNN_BLOCKS = 16
RNN_CONV = 4
LRU_C = 8.0
NSA_HEADS = 16
NSA_KV_HEADS = 4
HEAD_DIM = 64
GQA_REP = NSA_HEADS // NSA_KV_HEADS
CMP_BLOCK = 32
CMP_STRIDE = 16
CMP_HIDDEN = 128
SLC_BLOCK = 64
SLC_TOPK = 4
WINDOW = 256
Q_CHUNK = 64
FORCE_BONUS = 1.0e4
ROPE_THETA = 500000.0
ROPE_DIM = HEAD_DIM // 4
SC_WIDTH = D_MODEL
SC_CONV = 3
D_FF = 2816
FFN_CONV = 3
EPS = 1e-6
NEG = -1e30

AB_SPLITS = (RNN_WIDTH, RNN_WIDTH, NSA_HEADS * HEAD_DIM) + (NSA_KV_HEADS * HEAD_DIM,) * 6 + (3 * NSA_HEADS,)
AB_IN = sum(AB_SPLITS)
AB_MIX = RNN_WIDTH + NSA_HEADS * HEAD_DIM


def rms_norm(x, g):
    xf = x.astype(jnp.float32)
    y = xf * lax.rsqrt(jnp.mean(xf * xf, axis=-1, keepdims=True) + EPS)
    return (y * g.astype(jnp.float32)).astype(x.dtype)

def causal_dwconv(x, w, b):
    K, C = w.shape
    y = lax.conv_general_dilated(x, w[:, None, :].astype(x.dtype), window_strides=(1,),
                                 padding=[(K - 1, 0)], dimension_numbers=('NWC', 'WIO', 'NWC'),
                                 feature_group_count=C)
    return y + b.astype(x.dtype)

def rope_partial(x, pos):
    half = ROPE_DIM // 2
    inv = jnp.power(jnp.float32(ROPE_THETA), -jnp.arange(half, dtype=jnp.float32) / half)
    ang = pos.astype(jnp.float32)[:, None] * inv[None, :]
    cos = jnp.cos(ang)[None, :, None, :]
    sin = jnp.sin(ang)[None, :, None, :]
    x1 = x[..., :half].astype(jnp.float32)
    x2 = x[..., half:ROPE_DIM].astype(jnp.float32)
    rot = jnp.concatenate([x1 * cos - x2 * sin, x2 * cos + x1 * sin], axis=-1).astype(x.dtype)
    return jnp.concatenate([rot, x[..., ROPE_DIM:]], axis=-1)

def rg_lru(x, w_r, b_r, w_i, b_i, lam):
    Bsz, T, W = x.shape
    xb = x.reshape(Bsz, T, RNN_BLOCKS, W // RNN_BLOCKS)
    r = jax.nn.sigmoid(jnp.einsum('btnc,ncd->btnd', xb, w_r).reshape(Bsz, T, W) + b_r)
    i = jax.nn.sigmoid(jnp.einsum('btnc,ncd->btnd', xb, w_i).reshape(Bsz, T, W) + b_i)
    log_a = -LRU_C * r.astype(jnp.float32) * jax.nn.softplus(-lam.astype(jnp.float32))
    a = jnp.exp(log_a)
    u = jnp.sqrt(-jnp.expm1(2.0 * log_a)) * (i * x).astype(jnp.float32)

    def combine(left, right):
        a1, b1 = left
        a2, b2 = right
        return a1 * a2, a2 * b1 + b2

    _, h = lax.associative_scan(combine, (a, u), axis=1)
    return h.astype(x.dtype)

def compress(t, pe, w1, w2):
    Bsz, T, G, hd = t.shape
    n_cmp = (T - CMP_BLOCK) // CMP_STRIDE + 1
    idx = np.arange(n_cmp)[:, None] * CMP_STRIDE + np.arange(CMP_BLOCK)[None, :]
    blk = t[:, idx] + pe[:, None, :].astype(t.dtype)
    blk = blk.transpose(0, 1, 3, 2, 4).reshape(Bsz, n_cmp, G, CMP_BLOCK * hd)
    return jax.nn.gelu(blk @ w1) @ w2, idx[:, -1]

def nsa(q, kc, vc, ks, vs, kw, vw, gate_logits, pe_k, pe_v, wk1, wk2, wv1, wv2):
    Bsz, T = q.shape[:2]
    G, R, hd = NSA_KV_HEADS, GQA_REP, HEAD_DIM
    scale = HEAD_DIM ** -0.5
    pos = jnp.arange(T)
    q_rot = rope_partial(q, pos)
    ks = rope_partial(ks, pos)
    kw = rope_partial(kw, pos)
    k_cmp, cmp_end = compress(kc, pe_k, wk1, wk2)
    v_cmp, _ = compress(vc, pe_v, wv1, wv2)
    n_cmp = k_cmp.shape[1]
    cmp_end = jnp.asarray(cmp_end)
    n_slc = T // SLC_BLOCK
    k_sel = min(SLC_TOPK, n_slc)
    cs = np.arange(n_cmp) * CMP_STRIDE
    js = np.arange(n_slc) * SLC_BLOCK
    overlap = jnp.asarray(((cs[:, None] < js[None, :] + SLC_BLOCK) &
                           (cs[:, None] + CMP_BLOCK > js[None, :])).astype(np.float32))
    ksb = ks.reshape(Bsz, n_slc, SLC_BLOCK, G, hd).transpose(0, 3, 1, 2, 4)
    vsb = vs.reshape(Bsz, n_slc, SLC_BLOCK, G, hd).transpose(0, 3, 1, 2, 4)
    kwp = jnp.pad(kw, ((0, 0), (WINDOW, 0), (0, 0), (0, 0)))
    vwp = jnp.pad(vw, ((0, 0), (WINDOW, 0), (0, 0), (0, 0)))
    bi = jnp.arange(Bsz)[:, None, None, None]
    gi = jnp.arange(G)[None, :, None, None]
    blk_ids = jnp.arange(n_slc)
    f32 = jnp.float32

    def chunk(args):
        qn, qr, gt, s = args
        t = s + jnp.arange(Q_CHUNK)
        qn5 = qn.reshape(Bsz, Q_CHUNK, G, R, hd)
        qr5 = qr.reshape(Bsz, Q_CHUNK, G, R, hd)
        sc = jnp.einsum('bqgrd,bngd->bgrqn', qn5, k_cmp, preferred_element_type=f32) * scale
        mask_c = cmp_end[None, :] <= t[:, None]
        p_c = jnp.where(mask_c, jax.nn.softmax(jnp.where(mask_c, sc, NEG), axis=-1), 0.0)
        o_c = jnp.einsum('bgrqn,bngd->bqgrd', p_c.astype(v_cmp.dtype), v_cmp, preferred_element_type=f32)
        imp = jnp.einsum('bgrqn,nj->bgqj', p_c, overlap)
        forced = (blk_ids[None, :] == 0) | (blk_ids[None, :] == (t // SLC_BLOCK)[:, None])
        imp = jnp.where(forced, imp + FORCE_BONUS, imp)
        imp = jnp.where(blk_ids[None, :] * SLC_BLOCK <= t[:, None], imp, NEG)
        _, sel = lax.top_k(imp, k_sel)
        kg = ksb[bi, gi, sel]
        vg = vsb[bi, gi, sel]
        ss = jnp.einsum('bqgrd,bgqkld->bgrqkl', qr5, kg, preferred_element_type=f32) * scale
        tok = sel[..., None] * SLC_BLOCK + jnp.arange(SLC_BLOCK)
        mask_s = (tok <= t[None, None, :, None, None])[:, :, None]
        ss = jnp.where(mask_s, ss, NEG)
        p_s = jax.nn.softmax(ss.reshape(ss.shape[:4] + (k_sel * SLC_BLOCK,)), axis=-1).reshape(ss.shape)
        o_s = jnp.einsum('bgrqkl,bgqkld->bqgrd', p_s.astype(vg.dtype), vg, preferred_element_type=f32)
        kwin = lax.dynamic_slice_in_dim(kwp, s, WINDOW + Q_CHUNK, axis=1)
        vwin = lax.dynamic_slice_in_dim(vwp, s, WINDOW + Q_CHUNK, axis=1)
        j = s - WINDOW + jnp.arange(WINDOW + Q_CHUNK)
        mask_w = (j[None, :] <= t[:, None]) & (j[None, :] > t[:, None] - WINDOW) & (j[None, :] >= 0)
        sw = jnp.einsum('bqgrd,bjgd->bgrqj', qr5, kwin, preferred_element_type=f32) * scale
        p_w = jax.nn.softmax(jnp.where(mask_w, sw, NEG), axis=-1)
        o_w = jnp.einsum('bgrqj,bjgd->bqgrd', p_w.astype(vwin.dtype), vwin, preferred_element_type=f32)
        g = jax.nn.sigmoid(gt.astype(f32)).reshape(Bsz, Q_CHUNK, G, R, 3)
        o = g[..., 0:1] * o_c + g[..., 1:2] * o_s + g[..., 2:3] * o_w
        return o.reshape(Bsz, Q_CHUNK, NSA_HEADS * hd).astype(q.dtype)

    n_chunk = T // Q_CHUNK
    to_chunks = lambda a: a.reshape((Bsz, n_chunk, Q_CHUNK) + a.shape[2:]).swapaxes(0, 1)
    starts = jnp.arange(n_chunk) * Q_CHUNK
    out = lax.map(chunk, (to_chunks(q), to_chunks(q_rot), to_chunks(gate_logits), starts))
    return out.swapaxes(0, 1).reshape(Bsz, T, NSA_HEADS * hd)

def mixer_ab(h, w_in, conv_w, conv_b, w_r, b_r, w_i, b_i, lam, pe_k, pe_v, wk1, wk2, wv1, wv2, w_out):
    Bsz, T, _ = h.shape
    splits = np.cumsum(AB_SPLITS)[:-1].tolist()
    xr, gr, q, kc, vc, ks, vs, kw, vw, gl = jnp.split(h @ w_in, splits, axis=-1)
    y_rnn = rg_lru(causal_dwconv(xr, conv_w, conv_b), w_r, b_r, w_i, b_i, lam) * jax.nn.gelu(gr)
    kv = lambda a: a.reshape(Bsz, T, NSA_KV_HEADS, HEAD_DIM)
    y_att = nsa(q.reshape(Bsz, T, NSA_HEADS, HEAD_DIM), kv(kc), kv(vc), kv(ks), kv(vs), kv(kw), kv(vw),
                gl.reshape(Bsz, T, NSA_HEADS, 3), pe_k, pe_v, wk1, wk2, wv1, wv2)
    return jnp.concatenate([y_rnn, y_att], axis=-1) @ w_out

def mixer_c(h, w_in, conv_w, conv_b, w_out):
    bg, cg, v = jnp.split(h @ w_in, 3, axis=-1)
    return (bg * causal_dwconv(cg * v, conv_w, conv_b)) @ w_out

def conv_ffn(h, w_gate, w_up, conv_w, conv_b, w_down):
    g = causal_dwconv(h @ w_gate, conv_w, conv_b)
    return (jax.nn.silu(g) * (h @ w_up)) @ w_down

def first_inputs(seed: int = 0) -> dict:
    key = jax.random.key(seed)
    keys = iter(jax.random.split(key, 48))
    NE = (DEPTH + 1) // 2
    NO = DEPTH // 2
    f32 = jnp.float32

    def w(shape, fan_in, scale=1.0):
        return jax.random.normal(next(keys), shape, f32) * (scale * fan_in ** -0.5)

    def small(shape):
        return 0.02 * jax.random.normal(next(keys), shape, f32)

    def gain(shape):
        return 1.0 + small(shape)

    x = jax.random.normal(next(keys), (BATCH, SEQ, D_MODEL), f32)
    c = jax.random.normal(next(keys), (BATCH, D_MODEL), f32)
    a_target = jax.random.uniform(next(keys), (NE, RNN_WIDTH), f32, 0.9, 0.999)
    s = a_target ** (1.0 / LRU_C)
    lam = jnp.log(s) - jnp.log1p(-s)
    bw = RNN_WIDTH // RNN_BLOCKS
    return {
        'x': x,
        'c': c,
        'mod_w': w((DEPTH, D_MODEL, 6 * D_MODEL), D_MODEL, 0.5),
        'mod_b': small((DEPTH, 6 * D_MODEL)),
        'norm_mix_pre': gain((DEPTH, D_MODEL)),
        'norm_mix_post': gain((DEPTH, D_MODEL)),
        'norm_ffn_pre': gain((DEPTH, D_MODEL)),
        'norm_ffn_post': gain((DEPTH, D_MODEL)),
        'ab_w_in': w((NE, D_MODEL, AB_IN), D_MODEL),
        'ab_conv_w': w((NE, RNN_CONV, RNN_WIDTH), RNN_CONV),
        'ab_conv_b': small((NE, RNN_WIDTH)),
        'lru_w_r': w((NE, RNN_BLOCKS, bw, bw), bw),
        'lru_b_r': small((NE, RNN_WIDTH)),
        'lru_w_i': w((NE, RNN_BLOCKS, bw, bw), bw),
        'lru_b_i': small((NE, RNN_WIDTH)),
        'lru_lam': lam,
        'cmp_pe_k': small((NE, CMP_BLOCK, HEAD_DIM)),
        'cmp_pe_v': small((NE, CMP_BLOCK, HEAD_DIM)),
        'cmp_wk1': w((NE, CMP_BLOCK * HEAD_DIM, CMP_HIDDEN), CMP_BLOCK * HEAD_DIM),
        'cmp_wk2': w((NE, CMP_HIDDEN, HEAD_DIM), CMP_HIDDEN),
        'cmp_wv1': w((NE, CMP_BLOCK * HEAD_DIM, CMP_HIDDEN), CMP_BLOCK * HEAD_DIM),
        'cmp_wv2': w((NE, CMP_HIDDEN, HEAD_DIM), CMP_HIDDEN),
        'ab_w_out': w((NE, AB_MIX, D_MODEL), AB_MIX),
        'sc_w_in': w((NO, D_MODEL, 3 * SC_WIDTH), D_MODEL),
        'sc_conv_w': w((NO, SC_CONV, SC_WIDTH), SC_CONV),
        'sc_conv_b': small((NO, SC_WIDTH)),
        'sc_w_out': w((NO, SC_WIDTH, D_MODEL), SC_WIDTH),
        'ffn_w_gate': w((DEPTH, D_MODEL, D_FF), D_MODEL),
        'ffn_w_up': w((DEPTH, D_MODEL, D_FF), D_MODEL),
        'ffn_conv_w': w((DEPTH, FFN_CONV, D_FF), FFN_CONV),
        'ffn_conv_b': small((DEPTH, D_FF)),
        'ffn_w_down': w((DEPTH, D_FF, D_MODEL), D_FF),
    }

def first_block(x, c, mod_w, mod_b, norm_mix_pre, norm_mix_post, norm_ffn_pre, norm_ffn_post,
              ab_w_in, ab_conv_w, ab_conv_b, lru_w_r, lru_b_r, lru_w_i, lru_b_i, lru_lam,
              cmp_pe_k, cmp_pe_v, cmp_wk1, cmp_wk2, cmp_wv1, cmp_wv2, ab_w_out,
              sc_w_in, sc_conv_w, sc_conv_b, sc_w_out,
              ffn_w_gate, ffn_w_up, ffn_conv_w, ffn_conv_b, ffn_w_down):
    c_act = jax.nn.silu(c)
    for i in range(DEPTH):
        mod = c_act @ mod_w[i] + mod_b[i]
        sh_m, sc_m, g_m, sh_f, sc_f, g_f = jnp.split(mod[:, None, :], 6, axis=-1)
        h = rms_norm(x, norm_mix_pre[i]) * (1.0 + sc_m) + sh_m
        if i % 2 == 0:
            e = i // 2
            y = mixer_ab(h, ab_w_in[e], ab_conv_w[e], ab_conv_b[e], lru_w_r[e], lru_b_r[e],
                         lru_w_i[e], lru_b_i[e], lru_lam[e], cmp_pe_k[e], cmp_pe_v[e],
                         cmp_wk1[e], cmp_wk2[e], cmp_wv1[e], cmp_wv2[e], ab_w_out[e])
        else:
            o = i // 2
            y = mixer_c(h, sc_w_in[o], sc_conv_w[o], sc_conv_b[o], sc_w_out[o])
        x = x + (1.0 + g_m) * rms_norm(y, norm_mix_post[i])
        h = rms_norm(x, norm_ffn_pre[i]) * (1.0 + sc_f) + sh_f
        y = conv_ffn(h, ffn_w_gate[i], ffn_w_up[i], ffn_conv_w[i], ffn_conv_b[i], ffn_w_down[i])
        x = x + (1.0 + g_f) * rms_norm(y, norm_ffn_post[i])
    return x


GRID_W = 64
CTX_LEN = 256

MIX_W = D_MODEL
POOL_W = MIX_W // 2
POOL_GROUPS = 4
POOL_WINDOWS = (2, 4, 8, 16)
POOL_GC = POOL_W // POOL_GROUPS
MLA_HEADS = 8
QK_NOPE = 64
QK_ROPE = 32
V_HEAD = 64
Q_LORA = D_MODEL // 4
KV_LORA = D_MODEL // 4
IN_W = POOL_W + Q_LORA + KV_LORA + QK_ROPE
ROPE_AXIS = QK_ROPE // 2
ROPE_BASE = 10000.0
Q_BLOCK = 128
N_EXPERTS = 8
TOP_K = 2
D_FF_EXPERT = 3584
HY_WIDTH = D_MODEL
HY_SHORT = 3
HY_BANDS = 16
HY_EMB = 1 + 2 * HY_BANDS
HY_FILTER_HIDDEN = 64
HY_FAST_DECAY = 0.3
HY_SLOW_DECAY = 1.5
HY_TARGET = 1e-2
HY_MIN_DECAY = math.log(HY_TARGET) / HY_SLOW_DECAY
HY_MAX_DECAY = math.log(HY_TARGET) / HY_FAST_DECAY
LN_EPS = 1e-5
RMS_EPS = 1e-6


def layer_norm(x, g, b):
    xf = x.astype(jnp.float32)
    mu = jnp.mean(xf, axis=-1, keepdims=True)
    var = jnp.mean(jnp.square(xf - mu), axis=-1, keepdims=True)
    return ((xf - mu) * lax.rsqrt(var + LN_EPS) * g.astype(jnp.float32) + b.astype(jnp.float32)).astype(x.dtype)

def rms_norm_2(x, g):
    xf = x.astype(jnp.float32)
    return (xf * lax.rsqrt(jnp.mean(jnp.square(xf), axis=-1, keepdims=True) + RMS_EPS) * g.astype(jnp.float32)).astype(x.dtype)

def ada_chunks(s, w, b, k):
    mod = s @ w[:, :k * D_MODEL] + b[:k * D_MODEL]
    return [m[:, None, :] for m in jnp.split(mod, k, axis=-1)]

def axial_angles(n):
    rows = n // GRID_W
    r = jnp.repeat(jnp.arange(rows, dtype=jnp.float32), GRID_W)
    col = jnp.tile(jnp.arange(GRID_W, dtype=jnp.float32), rows)
    inv = ROPE_BASE ** (-jnp.arange(0, ROPE_AXIS, 2, dtype=jnp.float32) / ROPE_AXIS)
    return r[:, None] * inv, col[:, None] * inv

def rotate_pairs(x, ang):
    half = x.shape[-1] // 2
    x1, x2 = x[..., :half], x[..., half:]
    cos = jnp.cos(ang).astype(x.dtype)
    sin = jnp.sin(ang).astype(x.dtype)
    return jnp.concatenate([x1 * cos - x2 * sin, x2 * cos + x1 * sin], axis=-1)

def axial_rope(x, ang_r, ang_c):
    return jnp.concatenate([rotate_pairs(x[..., :ROPE_AXIS], ang_r), rotate_pairs(x[..., ROPE_AXIS:], ang_c)], axis=-1)

def multiscale_pool(u, pool_w, pool_scale):
    b, n, _ = u.shape
    ug = u.reshape(b, n, POOL_GROUPS, POOL_GC)
    cs = jnp.cumsum(ug.astype(jnp.float32), axis=1)
    cs = jnp.concatenate([jnp.zeros((b, 1, POOL_GROUPS, POOL_GC), jnp.float32), cs], axis=1)
    t = jnp.arange(n)[:, None]
    half = jnp.array([w // 2 for w in POOL_WINDOWS], dtype=jnp.int32)[None, :]
    lo = jnp.clip(t - half, 0, n)
    hi = jnp.clip(t + half, 0, n)
    grp = jnp.arange(POOL_GROUPS)[None, :]
    win_sum = cs[:, hi, grp] - cs[:, lo, grp]
    mean = win_sum / (hi - lo).astype(jnp.float32)[None, :, :, None]
    d = (mean - ug.astype(jnp.float32)).astype(u.dtype)
    y = jnp.einsum('bngc,gcd->bngd', d, pool_w)
    return y.reshape(b, n, POOL_W) * pool_scale

def mla_queries(q_lat, q_norm, q_up, ang):
    b, n, _ = q_lat.shape
    q = (rms_norm_2(q_lat, q_norm) @ q_up).reshape(b, n, MLA_HEADS, QK_NOPE + QK_ROPE)
    q_nope, q_rope = q[..., :QK_NOPE], q[..., QK_NOPE:]
    if ang is not None:
        q_rope = axial_rope(q_rope, ang[0][:, None, :], ang[1][:, None, :])
    return jnp.concatenate([q_nope, q_rope], axis=-1) * (QK_NOPE + QK_ROPE) ** -0.5

def mla_keys_values(kv_in, kv_norm, kv_up, ang):
    b, n, _ = kv_in.shape
    kv_lat, k_rope = kv_in[..., :KV_LORA], kv_in[..., KV_LORA:]
    kv = (rms_norm_2(kv_lat, kv_norm) @ kv_up).reshape(b, n, MLA_HEADS, QK_NOPE + V_HEAD)
    k_nope, v = kv[..., :QK_NOPE], kv[..., QK_NOPE:]
    if ang is not None:
        k_rope = axial_rope(k_rope, ang[0], ang[1])
    k = jnp.concatenate([k_nope, jnp.broadcast_to(k_rope[:, :, None, :], (b, n, MLA_HEADS, QK_ROPE))], axis=-1)
    return k, v

def attend(q, k, v):
    s = jnp.einsum('bqhd,bkhd->bhqk', q, k).astype(jnp.float32)
    p = jax.nn.softmax(s, axis=-1).astype(v.dtype)
    return jnp.einsum('bhqk,bkhd->bqhd', p, v)

def blocked_attend(q, k, v):
    b, n, h, d = q.shape
    qb = q.reshape(b, n // Q_BLOCK, Q_BLOCK, h, d).transpose(1, 0, 2, 3, 4)
    o = lax.map(lambda qq: attend(qq, k, v), qb)
    return o.transpose(1, 0, 2, 3, 4).reshape(b, n, h, V_HEAD)

def pool_mla_mixer(u, u_ctx, ctx_out, ang, in_w, pool_w, pool_scale, q_norm, q_up, kv_norm, kv_up, out_w):
    b, n, _ = u.shape
    kv0 = POOL_W + Q_LORA
    proj = u @ in_w
    if ctx_out:
        proj_c = u_ctx @ in_w
        kv_c_in = proj_c[..., kv0:]
    else:
        kv_c_in = u_ctx @ in_w[:, kv0:]
    k_c, v_c = mla_keys_values(kv_c_in, kv_norm, kv_up, None)
    k_l, v_l = mla_keys_values(proj[..., kv0:], kv_norm, kv_up, ang)
    q_l = mla_queries(proj[..., POOL_W:kv0], q_norm, q_up, ang)
    o_l = blocked_attend(q_l, jnp.concatenate([k_c, k_l], axis=1), jnp.concatenate([v_c, v_l], axis=1))
    y_l = jnp.concatenate([multiscale_pool(proj[..., :POOL_W], pool_w, pool_scale), o_l.reshape(b, n, MLA_HEADS * V_HEAD)], axis=-1) @ out_w
    y_c = None
    if ctx_out:
        m = u_ctx.shape[1]
        q_c = mla_queries(proj_c[..., POOL_W:kv0], q_norm, q_up, None)
        o_c = attend(q_c, k_c, v_c)
        y_c = jnp.concatenate([multiscale_pool(proj_c[..., :POOL_W], pool_w, pool_scale), o_c.reshape(b, m, MLA_HEADS * V_HEAD)], axis=-1) @ out_w
    return y_l, y_c

def short_conv(z, w, bias):
    y = lax.conv_general_dilated(z, w[:, None, :], window_strides=(1,), padding=[(HY_SHORT // 2, HY_SHORT // 2)],
                                 dimension_numbers=('NWC', 'WIO', 'NWC'), feature_group_count=z.shape[-1])
    return y + bias

def hyena_filters(n, fw1, fb1, fw2, fb2, fw3, fb3, fout, freq):
    t = jnp.linspace(0.0, 1.0, n, dtype=jnp.float32)[:, None]
    w_ang = (2.0 * math.pi / n) * jnp.arange(n, dtype=jnp.float32)[:, None]
    bands = jnp.linspace(1e-4, HY_BANDS - 1, HY_BANDS, dtype=jnp.float32)[None, :]
    z = jnp.concatenate([t, jnp.cos(bands * w_ang), -jnp.sin(bands * w_ang)], axis=-1)
    freq = freq.astype(jnp.float32)
    h = jnp.sin(freq * (z @ fw1.astype(jnp.float32) + fb1.astype(jnp.float32)))
    h = jnp.sin(freq * (h @ fw2.astype(jnp.float32) + fb2.astype(jnp.float32)))
    h = jnp.sin(freq * (h @ fw3.astype(jnp.float32) + fb3.astype(jnp.float32)))
    h = (h @ fout.astype(jnp.float32)).reshape(n, 2, HY_WIDTH)
    deltas = jnp.abs(jnp.linspace(HY_MIN_DECAY, HY_MAX_DECAY, HY_WIDTH, dtype=jnp.float32))
    h = h * jnp.exp(-t * deltas)[:, None, :]
    return h[:, 0], h[:, 1]

def bidir_long_conv(v, h_f, h_b, skip):
    b, n, ch = v.shape
    vf = v.astype(jnp.float32)
    k = jnp.concatenate([h_f, jnp.zeros((1, ch), jnp.float32), jnp.flip(h_b[1:], axis=0)], axis=0)
    spec = jnp.fft.rfft(vf, n=2 * n, axis=1) * jnp.fft.rfft(k, n=2 * n, axis=0)[None]
    y = jnp.fft.irfft(spec, n=2 * n, axis=1)[:, :n]
    return (y + vf * skip.astype(jnp.float32)).astype(v.dtype)

def hyena_mixer(u, in_w, conv_w, conv_b, fw1, fb1, fw2, fb2, fw3, fb3, fout, freq, skip, out_w):
    n = u.shape[1]
    z = short_conv(u @ in_w, conv_w, conv_b)
    x0, x1, v = jnp.split(z, 3, axis=-1)
    h_f, h_b = hyena_filters(n, fw1, fb1, fw2, fb2, fw3, fb3, fout, freq)
    y = x0 * bidir_long_conv(v * x1, h_f, h_b, skip)
    return y @ out_w

def swiglu(h, wg, wu, wd):
    return (jax.nn.silu(h @ wg) * (h @ wu)) @ wd

def moe_swiglu(h, router_w, wg, wu, wd):
    shp = h.shape
    t = h.reshape(-1, shp[-1])
    logits = (t @ router_w).astype(jnp.float32)
    top_v, top_i = lax.top_k(logits, TOP_K)
    gates = jax.nn.softmax(top_v, axis=-1)
    combine = jnp.sum(jax.nn.one_hot(top_i, N_EXPERTS, dtype=jnp.float32) * gates[..., None], axis=1).astype(h.dtype)
    out = jnp.zeros_like(t)
    for e in range(N_EXPERTS):
        out = out + combine[:, e:e + 1] * swiglu(t, wg[e], wu[e], wd[e])
    return out.reshape(shp)

def second_inputs(seed: int = 0) -> dict:
    key = jax.random.key(seed)
    keys = jax.random.split(key, 48)
    counter = [0]

    def nrm(shape, scale):
        k = keys[counter[0]]
        counter[0] += 1
        return jax.random.normal(k, shape, jnp.float32) * scale

    D = D_MODEL
    ne = (DEPTH + 1) // 2
    no = DEPTH // 2
    beta = (8.0 * DEPTH) ** -0.25
    fh = HY_FILTER_HIDDEN
    return {
        'x': nrm((BATCH, SEQ, D), 1.0),
        'c': nrm((BATCH, D), 1.0),
        'ctx': nrm((BATCH, CTX_LEN, D), 1.0),
        'c_ctx': nrm((D,), 1.0),
        'ada_w': nrm((DEPTH, D, 6 * D), 0.5 * D ** -0.5),
        'ada_b': nrm((DEPTH, 6 * D), 0.02),
        'ln_g': 1.0 + nrm((DEPTH, 2, D), 0.02),
        'ln_b': nrm((DEPTH, 2, D), 0.02),
        'mix_in_w': nrm((ne, D, IN_W), D ** -0.5),
        'pool_w': nrm((ne, POOL_GROUPS, POOL_GC, POOL_GC), POOL_GC ** -0.5),
        'pool_scale': 1.0 + nrm((ne, POOL_W), 0.02),
        'q_norm': 1.0 + nrm((ne, Q_LORA), 0.02),
        'q_up': nrm((ne, Q_LORA, MLA_HEADS * (QK_NOPE + QK_ROPE)), Q_LORA ** -0.5),
        'kv_norm': 1.0 + nrm((ne, KV_LORA), 0.02),
        'kv_up': nrm((ne, KV_LORA, MLA_HEADS * (QK_NOPE + V_HEAD)), KV_LORA ** -0.5),
        'mix_out_w': nrm((ne, MIX_W, D), beta * MIX_W ** -0.5),
        'ffn_gate': nrm((ne, D, D_FF), D ** -0.5),
        'ffn_up': nrm((ne, D, D_FF), D ** -0.5),
        'ffn_down': nrm((ne, D_FF, D), beta * D_FF ** -0.5),
        'hy_in_w': nrm((no, D, 3 * HY_WIDTH), D ** -0.5),
        'hy_conv_w': nrm((no, HY_SHORT, 3 * HY_WIDTH), HY_SHORT ** -0.5),
        'hy_conv_b': nrm((no, 3 * HY_WIDTH), 0.02),
        'hy_fw1': nrm((no, HY_EMB, fh), HY_EMB ** -0.5),
        'hy_fb1': nrm((no, fh), 0.1),
        'hy_fw2': nrm((no, fh, fh), fh ** -0.5),
        'hy_fb2': nrm((no, fh), 0.1),
        'hy_fw3': nrm((no, fh, fh), fh ** -0.5),
        'hy_fb3': nrm((no, fh), 0.1),
        'hy_fout': nrm((no, fh, 2 * HY_WIDTH), 0.1 * fh ** -0.5),
        'hy_freq': 1.0 + nrm((no, fh), 0.02),
        'hy_skip': nrm((no, HY_WIDTH), 1.0),
        'hy_out_w': nrm((no, HY_WIDTH, D), beta * HY_WIDTH ** -0.5),
        'router_w': nrm((no, D, N_EXPERTS), D ** -0.5),
        'moe_gate': nrm((no, N_EXPERTS, D, D_FF_EXPERT), D ** -0.5),
        'moe_up': nrm((no, N_EXPERTS, D, D_FF_EXPERT), D ** -0.5),
        'moe_down': nrm((no, N_EXPERTS, D_FF_EXPERT, D), beta * D_FF_EXPERT ** -0.5),
    }

def second_block(x, c, ctx, c_ctx, ada_w, ada_b, ln_g, ln_b, mix_in_w, pool_w, pool_scale, q_norm, q_up, kv_norm, kv_up,
              mix_out_w, ffn_gate, ffn_up, ffn_down, hy_in_w, hy_conv_w, hy_conv_b, hy_fw1, hy_fb1, hy_fw2, hy_fb2,
              hy_fw3, hy_fb3, hy_fout, hy_freq, hy_skip, hy_out_w, router_w, moe_gate, moe_up, moe_down):
    alpha = (2.0 * DEPTH) ** 0.25
    n = x.shape[1]
    ang = axial_angles(n)
    s_lat = jax.nn.silu(c)
    s_ctx = jax.nn.silu(c_ctx)[None, :]
    last_reader = (DEPTH - 1) - ((DEPTH - 1) % 2)
    h, hc = x, ctx
    for l in range(DEPTH):
        i = l // 2
        even = (l % 2 == 0)
        ctx_live = l <= last_reader
        ctx_out = l < last_reader
        sh1, sc1, g1, sh2, sc2, g2 = ada_chunks(s_lat, ada_w[l], ada_b[l], 6)
        u = h * (1 + sc1) + sh1
        uc, mc = None, None
        if ctx_live:
            mc = ada_chunks(s_ctx, ada_w[l], ada_b[l], 6 if ctx_out else 2)
            uc = hc * (1 + mc[1]) + mc[0]
        if even:
            y, yc = pool_mla_mixer(u, uc, ctx_out, ang, mix_in_w[i], pool_w[i], pool_scale[i], q_norm[i], q_up[i],
                                   kv_norm[i], kv_up[i], mix_out_w[i])
        else:
            hy_args = (hy_in_w[i], hy_conv_w[i], hy_conv_b[i], hy_fw1[i], hy_fb1[i], hy_fw2[i], hy_fb2[i],
                       hy_fw3[i], hy_fb3[i], hy_fout[i], hy_freq[i], hy_skip[i], hy_out_w[i])
            y = hyena_mixer(u, *hy_args)
            yc = hyena_mixer(uc, *hy_args) if ctx_out else None

        def channel_mix(z):
            if even:
                return swiglu(z, ffn_gate[i], ffn_up[i], ffn_down[i])
            return moe_swiglu(z, router_w[i], moe_gate[i], moe_up[i], moe_down[i])

        h = layer_norm(alpha * h + g1 * y, ln_g[l, 0], ln_b[l, 0])
        h = layer_norm(alpha * h + g2 * channel_mix(h * (1 + sc2) + sh2), ln_g[l, 1], ln_b[l, 1])
        if ctx_out:
            hc = layer_norm(alpha * hc + mc[2] * yc, ln_g[l, 0], ln_b[l, 0])
            hc = layer_norm(alpha * hc + mc[5] * channel_mix(hc * (1 + mc[4]) + mc[3]), ln_g[l, 1], ln_b[l, 1])
    return h


def setup_inputs(seed=0):
    out = dict(first_inputs(seed))
    for name, value in second_inputs(seed + 1).items():
        if name != "x":
            out[name + "_2"] = value
    return out


def reference(
    x, c, mod_w, mod_b, norm_mix_pre, norm_mix_post, norm_ffn_pre, norm_ffn_post, ab_w_in,
    ab_conv_w, ab_conv_b, lru_w_r, lru_b_r, lru_w_i, lru_b_i, lru_lam, cmp_pe_k, cmp_pe_v,
    cmp_wk1, cmp_wk2, cmp_wv1, cmp_wv2, ab_w_out, sc_w_in, sc_conv_w, sc_conv_b, sc_w_out,
    ffn_w_gate, ffn_w_up, ffn_conv_w, ffn_conv_b, ffn_w_down, c_2, ctx_2, c_ctx_2, ada_w_2,
    ada_b_2, ln_g_2, ln_b_2, mix_in_w_2, pool_w_2, pool_scale_2, q_norm_2, q_up_2, kv_norm_2,
    kv_up_2, mix_out_w_2, ffn_gate_2, ffn_up_2, ffn_down_2, hy_in_w_2, hy_conv_w_2, hy_conv_b_2,
    hy_fw1_2, hy_fb1_2, hy_fw2_2, hy_fb2_2, hy_fw3_2, hy_fb3_2, hy_fout_2, hy_freq_2, hy_skip_2,
    hy_out_w_2, router_w_2, moe_gate_2, moe_up_2, moe_down_2,
):
    x = first_block(
        x, c, mod_w, mod_b, norm_mix_pre, norm_mix_post, norm_ffn_pre, norm_ffn_post, ab_w_in,
        ab_conv_w, ab_conv_b, lru_w_r, lru_b_r, lru_w_i, lru_b_i, lru_lam, cmp_pe_k, cmp_pe_v,
        cmp_wk1, cmp_wk2, cmp_wv1, cmp_wv2, ab_w_out, sc_w_in, sc_conv_w, sc_conv_b, sc_w_out,
        ffn_w_gate, ffn_w_up, ffn_conv_w, ffn_conv_b, ffn_w_down,
    )
    return second_block(
        x, c_2, ctx_2, c_ctx_2, ada_w_2, ada_b_2, ln_g_2, ln_b_2, mix_in_w_2, pool_w_2,
        pool_scale_2, q_norm_2, q_up_2, kv_norm_2, kv_up_2, mix_out_w_2, ffn_gate_2, ffn_up_2,
        ffn_down_2, hy_in_w_2, hy_conv_w_2, hy_conv_b_2, hy_fw1_2, hy_fb1_2, hy_fw2_2, hy_fb2_2,
        hy_fw3_2, hy_fb3_2, hy_fout_2, hy_freq_2, hy_skip_2, hy_out_w_2, router_w_2, moe_gate_2,
        moe_up_2, moe_down_2,
    )


_drawn_inputs = setup_inputs


def setup_inputs(seed=0):
    import zlib

    import numpy as np

    out = dict(_drawn_inputs(seed))
    spreads = {}
    factors = {'norm_ffn_post': 3.023,
     'lru_b_r': 8.0,
     'lru_b_i': 6.581,
     'cmp_pe_k': 8.0,
     'cmp_pe_v': 7.321,
     'sc_conv_b': 5.784,
     'ffn_conv_b': 3.211,
     'ctx_2': 8.0,
     'c_ctx_2': 8.0,
     'ada_b_2': 3.625,
     'pool_scale_2': 50.67,
     'q_norm_2': 8.0,
     'q_up_2': 8.0,
     'kv_norm_2': 8.0,
     'kv_up_2': 5.479,
     'hy_conv_b_2': 8.0,
     'hy_fb1_2': 6.082,
     'hy_fb2_2': 5.454,
     'hy_fb3_2': 3.773,
     'hy_freq_2': 8.0}
    for name, (base, spread) in spreads.items():
        noise = np.random.default_rng([zlib.crc32(name.encode()), seed]).standard_normal(out[name].shape)
        drawn = base * np.exp(spread * noise) if base else spread * noise
        out[name] = __import__('jax').numpy.asarray(drawn.astype(out[name].dtype))
    for name, factor in factors.items():
        out[name] = (out[name] * factor).astype(out[name].dtype)
    return out
```

```python
import math
from contextlib import ExitStack

import numpy as np

import concourse.bass as bass
from concourse import mybir

F32 = mybir.dt.float32
U32 = mybir.dt.uint32
ALU = mybir.AluOpType
ACT = mybir.ActivationFunctionType
AX = mybir.AxisListType

P = 128
T = 256
D = 1024
KT = D // P
TILES = 32
CH = TILES * P
RING = 7
BANKS = 8
NEG = -1e30

HEADS, KVH, HD, REP = 16, 4, 64, 4
NCMP, CMPB, CMPS = 15, 32, 16
FF, FT = 2816, 22
MH, NOPE, ROPE, VH = 8, 64, 32, 64
EXPERTS, FE = 8, 3584
FEJ = FE // 512
EXTRA = (2 * T - 1) // (P + 1)
NF = 512
EPS_RMS, EPS_LN = 1e-6, 1e-5
ALPHA = (2.0 * 2) ** 0.25


def column_plan():
    names = [("c", 8), ("c_ctx", 8), ("c2", 8), ("mod_b", 4 * 48),
             ("g_mix_pre", 16), ("g_mix_post", 16), ("g_ffn_pre", 16), ("g_ffn_post", 16),
             ("ab_conv_w", 32), ("ab_conv_b", 8), ("lru_b_r", 8), ("lru_b_i", 8), ("lru_lam", 8),
             ("pe_t", 32), ("sc_conv_w", 24), ("sc_conv_b", 8),
             ("ffn_conv_w", 2 * 3 * FT), ("ffn_conv_b", 2 * FT),
             ("ln_g", 32), ("ln_b", 32), ("pool_scale", 4), ("q_norm", 2), ("kv_norm", 2),
             ("hy_conv_w", 72), ("hy_conv_b", 24), ("hy_fb", 3), ("hy_freq", 1), ("hy_skip", 8),
             ("router", 64), ("fw", 3 * 64), ("z_t", T), ("iota", EXPERTS), ("wk2", P), ("wv2", HD)]
    at, out = 0, {}
    for n, w in names:
        out[n] = (at, w)
        at += w
    return out, at


COL, NCOL = column_plan()


def const_plan():
    names = [("ident", P), ("ones", P), ("rope_r", P), ("rope_cos", T), ("rope_sin", T),
             ("causal", T), ("cmp_neg", 2 * NCMP), ("cmp_one", 2 * NCMP),
             ("mla_r", 96), ("mla_cos", T), ("mla_sin", T), ("kr_cos", T), ("kr_sin", T), ("kr_r", 32),
             ("earlier", P), ("slots", P)]
    at, out = 0, {}
    for n, w in names:
        out[n] = (at, w)
        at += w
    return out, at


CCOL, NCONST = const_plan()

def stage_list():
    s = ["D"] * 4
    s += [64, "D", "D", 64, "D", "D", 32, "D", 64, "D", 32, "D", 32, "D", 32, 32, 128]
    s += [x for j in range(11) for x in (32, "D")] + [44, "D", 132]
    s += [x for j in range(4) for x in (48, "D", "D")] + [64]
    s += [x for j in range(11) for x in (32, "D")] + [44, "D", 132]
    s += [112, 64]
    s += [x for j in range(11) for x in ((32, "D") if j < 4 else (32,))] + [176]
    s += [16, 192, 64]
    return s


def chunk_plan():
    kinds, open_tiles, waiting = [], 0, 0
    for s in stage_list():
        if s == "D":
            if open_tiles:
                waiting += 1
            else:
                kinds.append("D")
            continue
        for _ in range(s):
            if open_tiles == 0:
                kinds.append("P")
            open_tiles = (open_tiles + 1) % TILES
            if open_tiles == 0:
                kinds += ["D"] * waiting
                waiting = 0
    kinds += ["D"] * waiting
    return kinds


KINDS = chunk_plan()
P_CHUNKS = [i for i, k in enumerate(KINDS) if k == "P"]
D_CHUNKS = [i for i, k in enumerate(KINDS) if k == "D"]
assert len(D_CHUNKS) == 48, len(D_CHUNKS)
MOE_BASE = len(KINDS)
N_TILES = sum(s for s in stage_list() if s != "D")


def expert_chunk(kind, j):
    if kind < 2:
        return (2 * j if j < 2 else 3 * j - 2) + kind
    return min(3 * j + 6, 2 * FEJ + j)


def lhs_tiles(w, width=P):
    k, m = w.shape
    return w.reshape(k // P, P, m // width, width).transpose(2, 0, 1, 3).reshape(-1, P, width)


def rhs_tiles(w):
    k, n = w.shape
    return w.reshape(k // P, P, n // P, P).transpose(0, 2, 1, 3).reshape(-1, P, P)


def flat_tiles(a):
    n = -(-a.shape[1] // P) * P
    out = np.zeros((P, n), np.float32)
    out[:a.shape[0], :a.shape[1]] = a
    return out.reshape(P, n // P, P).transpose(1, 0, 2)


def cols(v):
    v = np.ascontiguousarray(v).reshape(-1, P)
    return v.T


def q_order():
    heads = [4 * (2 * gp + half) + r for gp in range(2) for r in range(4) for half in range(2)]
    return np.concatenate([np.arange(h * HD, (h + 1) * HD) for h in heads])


def dft_tables():
    t = np.arange(T)[:, None]
    f = np.arange(T)[None, :]
    ang = 2 * np.pi * ((t * f) % NF) / NF
    co, si = np.cos(ang), -np.sin(ang)
    fwd = np.concatenate([co, si], 1)
    fwd[:, T] = (-1.0) ** t[:, 0]
    back = np.concatenate([co, -si], 1)
    back[:, T] = (-1.0) ** t[:, 0]
    back[0, :] = 0.0
    wc, ws = 2 * np.cos(ang).T / NF, -2 * np.sin(ang).T / NF
    wc[0] = 1.0 / NF
    ws[0] = ((-1.0) ** t[:, 0]) / NF
    inv = np.concatenate([wc, ws], 0)
    return fwd.astype(np.float32), back.astype(np.float32), inv.astype(np.float32)


def rotation(n, pairs):
    r = np.zeros((n, n), np.float32)
    for a, b in pairs:
        r[b, a] = -1.0
        r[a, b] = 1.0
    return r


def host_consts():
    c = np.zeros((P, NCONST), np.float32)

    def put(name, a):
        at, w = CCOL[name]
        assert a.shape[1] == w, name
        c[:a.shape[0], at:at + w] = a

    put("ident", np.eye(P, dtype=np.float32))
    put("ones", np.ones((P, P), np.float32))
    half = 8
    pairs = [(o + i, o + half + i) for o in (0, 64) for i in range(half)]
    put("rope_r", rotation(P, pairs))
    inv = np.power(np.float32(500000.0), -np.arange(half, dtype=np.float32) / np.float32(half)).astype(np.float32)
    ang = np.arange(T, dtype=np.float32)[:, None] * inv[None, :]
    co, si = np.ones((P, T), np.float32), np.zeros((P, T), np.float32)
    for o in (0, 64):
        for h in (0, half):
            co[o + h:o + h + half] = np.cos(ang).T
            si[o + h:o + h + half] = np.sin(ang).T
    put("rope_cos", co)
    put("rope_sin", si)
    i = np.arange(P)
    causal = np.where(i[None, :] <= i[:, None], 0.0, NEG).astype(np.float32)
    put("causal", np.concatenate([np.zeros_like(causal), causal], 1))
    tt = np.arange(T)[:, None]
    ok = (np.arange(NCMP)[None, :] * CMPS + CMPB - 1) <= tt
    ok = ok.reshape(2, P, NCMP).transpose(1, 0, 2).reshape(P, 2 * NCMP)
    put("cmp_neg", np.where(ok, 0.0, NEG).astype(np.float32))
    put("cmp_one", ok.astype(np.float32))
    ax = ROPE // 2
    inv2 = (10000.0 ** (-np.arange(0, ax, 2, dtype=np.float32) / ax)).astype(np.float32)
    rows = np.repeat(np.arange(T // 64, dtype=np.float32), 64)
    colp = np.tile(np.arange(64, dtype=np.float32), T // 64)
    ar, ac = rows[:, None] * inv2, colp[:, None] * inv2
    kc, ks = np.zeros((ROPE, T), np.float32), np.zeros((ROPE, T), np.float32)
    for o, a in ((0, ar), (16, ac)):
        for h in (0, 8):
            kc[o + h:o + h + 8] = np.cos(a).T
            ks[o + h:o + h + 8] = np.sin(a).T
    kp = [(o + i, o + 8 + i) for o in (0, 16) for i in range(8)]
    put("kr_cos", kc)
    put("kr_sin", ks)
    put("kr_r", rotation(ROPE, kp))
    mc, ms = np.ones((96, T), np.float32), np.zeros((96, T), np.float32)
    mc[NOPE:], ms[NOPE:] = kc, ks
    put("mla_cos", mc)
    put("mla_sin", ms)
    put("earlier", np.triu(np.ones((P, P), np.float32), 1))
    put("slots", np.tile(np.arange(P, dtype=np.float32)[None], (P, 1)))
    put("mla_r", rotation(96, [(NOPE + a, NOPE + b) for a, b in kp]))
    return c


def pool_matrix():
    t = np.arange(T)
    out = np.zeros((T, 4, T), np.float32)
    for g, w in enumerate((2, 4, 8, 16)):
        lo, hi = np.clip(t - w // 2, 0, T), np.clip(t + w // 2, 0, T)
        for a in range(T):
            out[lo[a]:hi[a], g, a] = np.float32(1.0) / np.float32(hi[a] - lo[a])
        out[t, g, t] -= 1.0
    return out


def hyena_tables():
    n = T
    t = np.linspace(0.0, 1.0, n, dtype=np.float32)[:, None]
    w_ang = np.float32(2.0 * math.pi / n) * np.arange(n, dtype=np.float32)[:, None]
    bands = np.linspace(1e-4, 15, 16, dtype=np.float32)[None, :]
    z = np.concatenate([t, np.cos(bands * w_ang), -np.sin(bands * w_ang)], axis=-1).astype(np.float32)
    lo, hi = math.log(1e-2) / 1.5, math.log(1e-2) / 0.3
    deltas = np.abs(np.linspace(lo, hi, D, dtype=np.float32))
    return z, np.exp(-t * deltas).astype(np.float32)


def host_layout(a):
    vec = np.zeros((P, NCOL), np.float32)

    def put(name, x):
        at, w = COL[name]
        assert x.shape[1] == w, (name, x.shape)
        vec[:x.shape[0], at:at + w] = x

    put("c", cols(a["c"]))
    put("c_ctx", cols(a["c_ctx_2"]))
    put("c2", cols(a["c_2"]))
    put("mod_b", np.concatenate([cols(a["mod_b"]), cols(a["ada_b_2"])], 1))
    for n, k in (("g_mix_pre", "norm_mix_pre"), ("g_mix_post", "norm_mix_post"), ("g_ffn_pre", "norm_ffn_pre"),
                 ("g_ffn_post", "norm_ffn_post"), ("ab_conv_w", "ab_conv_w"), ("ab_conv_b", "ab_conv_b"),
                 ("lru_b_r", "lru_b_r"), ("lru_b_i", "lru_b_i"), ("lru_lam", "lru_lam"),
                 ("sc_conv_w", "sc_conv_w"), ("sc_conv_b", "sc_conv_b"), ("ffn_conv_w", "ffn_conv_w"),
                 ("ffn_conv_b", "ffn_conv_b"), ("ln_g", "ln_g_2"), ("ln_b", "ln_b_2"),
                 ("pool_scale", "pool_scale_2"), ("q_norm", "q_norm_2"), ("kv_norm", "kv_norm_2"),
                 ("hy_conv_w", "hy_conv_w_2"), ("hy_conv_b", "hy_conv_b_2"), ("hy_skip", "hy_skip_2")):
        put(n, cols(a[k]))
    put("pe_t", np.concatenate([a["cmp_pe_k"][0].T, a["cmp_pe_v"][0].T], 0))
    put("hy_fb", np.stack([a["hy_fb1_2"][0], a["hy_fb2_2"][0], a["hy_fb3_2"][0]], 1))
    put("hy_freq", a["hy_freq_2"][0][:, None])
    put("router", a["router_w_2"][0].reshape(KT, P, EXPERTS).transpose(1, 0, 2).reshape(P, -1))
    fw = np.zeros((64, 3 * 64), np.float32)
    fw[:33, :64] = a["hy_fw1_2"][0]
    fw[:, 64:128] = a["hy_fw2_2"][0]
    fw[:, 128:] = a["hy_fw3_2"][0]
    put("fw", fw)
    z, decay = hyena_tables()
    put("z_t", np.ascontiguousarray(z.T))
    put("iota", np.tile(np.arange(EXPERTS, dtype=np.float32)[None], (P, 1)))

    put("wk2", np.concatenate([a["cmp_wk2"][0], a["cmp_wk2"][0]], 1))
    put("wv2", a["cmp_wv2"][0])

    tiles = []
    w = a["ab_w_in"][0]
    off = np.cumsum([0, 1024, 1024, 1024] + [256] * 6 + [48])
    xr, gr, q, kc, vc, ks, vs, kw, vw, gl = (w[:, off[i]:off[i + 1]] for i in range(10))
    kcvc = np.concatenate([x[:, g * HD:(g + 1) * HD] for g in range(KVH) for x in (kc, vc)], 1)
    misc = [flat_tiles(gl.reshape(KT, P, 48).transpose(1, 0, 2).reshape(P, -1))]
    for n in ("lru_w_r", "lru_w_i"):
        bd = np.zeros((KT, P, P), np.float32)
        for m in range(KT):
            bd[m, :64, :64] = a[n][0, 2 * m]
            bd[m, 64:, 64:] = a[n][0, 2 * m + 1]
        misc.append(bd)
    misc.append(np.zeros((TILES - 19, P, P), np.float32))
    tiles += [lhs_tiles(xr), lhs_tiles(gr)] + misc
    tiles += [lhs_tiles(q[:, q_order()]), lhs_tiles(kcvc),
              lhs_tiles(np.concatenate([ks, kw], 1)), rhs_tiles(np.concatenate([vs, vw], 1))]
    w1 = [a[n][0].reshape(CMPB, HD, P) for n in ("cmp_wk1", "cmp_wv1")]
    tiles.append(np.concatenate(w1, 1))
    tiles.append(lhs_tiles(a["ab_w_out"][0]))

    def ffn(wg, wu, wd):
        g, u = lhs_tiles(wg), lhs_tiles(wu)
        for j in range(FT // 2):
            tiles.append(g[16 * j:16 * j + 16])
            tiles.append(u[16 * j:16 * j + 16])
        tiles.append(lhs_tiles(wd))

    ffn(a["ffn_w_gate"][0], a["ffn_w_up"][0], a["ffn_w_down"][0])
    sc = lhs_tiles(a["sc_w_in"][0]).reshape(3, 4, 16, P, P)
    for j in range(4):
        tiles += [sc[1, j], sc[2, j], sc[0, j]]
    tiles.append(lhs_tiles(a["sc_w_out"][0]))
    ffn(a["ffn_w_gate"][1], a["ffn_w_up"][1], a["ffn_w_down"][1])
    mi = a["mix_in_w_2"][0]
    tiles.append(rhs_tiles(mi[:, :512]))
    tiles.append(lhs_tiles(mi[:, 512:1024]))
    krw = mi[:, 1024:1056].reshape(KT, P, 32).transpose(1, 0, 2).reshape(P, -1)
    tiles.append(flat_tiles(krw))
    qu = a["q_up_2"][0].reshape(2, P, MH, 96).transpose(1, 2, 0, 3).reshape(P, -1)
    tiles.append(flat_tiles(qu))
    kvu = a["kv_up_2"][0].reshape(2, P, MH, 128)
    tiles.append(flat_tiles(np.ascontiguousarray(kvu[..., :64].transpose(1, 2, 0, 3)).reshape(P, -1)))
    tiles.append(flat_tiles(np.ascontiguousarray(kvu[..., 64:].transpose(1, 0, 2, 3)).reshape(P, -1)))
    tiles.append(a["pool_w_2"][0])
    tiles.append(np.zeros((112 - (32 + 32 + 2 + 12 + 8 + 8 + 4), P, P), np.float32))
    tiles.append(lhs_tiles(a["mix_out_w_2"][0]))
    ffn(a["ffn_gate_2"][0], a["ffn_up_2"][0], a["ffn_down_2"][0])
    tiles.append(flat_tiles(a["hy_fout_2"][0]))
    hy = lhs_tiles(a["hy_in_w_2"][0]).reshape(3, 4, 16, P, P)
    for j in range(4):
        tiles += [hy[1, j], hy[2, j], hy[0, j]]
    tiles.append(lhs_tiles(a["hy_out_w_2"][0]))
    tiles = np.concatenate(tiles, 0)
    assert tiles.shape[0] == N_TILES, (tiles.shape, N_TILES)

    n_chunks = MOE_BASE + EXPERTS * FEJ * 3
    stream = np.zeros((n_chunks, P, CH), np.float32)
    for n, c in enumerate(P_CHUNKS):
        t = tiles[TILES * n:TILES * n + TILES]
        stream[c, :, :t.shape[0] * P] = t.transpose(1, 0, 2).reshape(P, -1)
    mods = [a["mod_w"][0], a["mod_w"][1], a["ada_w_2"][0], a["ada_w_2"][1]]
    for n, c in enumerate(D_CHUNKS):
        blk = mods[n // 12][:, 512 * (n % 12):512 * (n % 12) + 512]
        stream[c] = blk.reshape(KT, P, 512).transpose(1, 0, 2).reshape(P, CH)
    moe = stream[MOE_BASE:].reshape(EXPERTS, 3 * FEJ, P, CH)
    at = [[expert_chunk(i, j) for j in range(FEJ)] for i in range(3)]
    for s, n in ((0, "moe_gate_2"), (1, "moe_up_2")):
        moe[:, at[s]] = a[n][0].reshape(EXPERTS, KT, P, FEJ, 512).transpose(0, 3, 2, 1, 4).reshape(EXPERTS, FEJ, P, CH)
    moe[:, at[2]] = a["moe_down_2"][0].reshape(EXPERTS, FEJ, 4, P, D).transpose(0, 1, 3, 2, 4).reshape(EXPERTS, FEJ, P, CH)

    fwd, back, inv = dft_tables()
    def token_tiles(x):
        return x.reshape(-1, P, x.shape[1]).transpose(1, 0, 2).reshape(P, -1)
    tables = np.concatenate([token_tiles(fwd), token_tiles(back), token_tiles(inv), token_tiles(decay),
                             token_tiles(pool_matrix().reshape(T, 4 * T))], 1)
    x_t = np.ascontiguousarray(a["x"][0].T).reshape(KT, P, T).transpose(1, 0, 2)
    ctx_t = np.ascontiguousarray(a["ctx_2"][0].T).reshape(KT, P, T).transpose(1, 0, 2)
    return {"stream": stream, "vecs": vec, "consts": host_consts(), "tables": np.ascontiguousarray(tables),
            "x_t": np.ascontiguousarray(x_t), "ctx_t": np.ascontiguousarray(ctx_t)}


def ffn_products(tag, conv, mods):
    out = []
    for j in range(FT // 2):
        out += [(f"gate{tag}", j), (f"up{tag}", j)]
        if 0 <= j - 1 < mods:
            out.append(("mod", None))
    out.append((f"down{tag}", 0))
    if mods >= 11:
        out.append(("mod", None))
    out.append((f"down{tag}", 1))
    if mods == 12:
        out.append(("mod", None))
    return out + [(f"down{tag}", 2), (f"down{tag}", 3)]


def attention_order(tag, units):
    out = []
    for i in range(units + 3):
        if i < units:
            out.append((f"{tag}_scores", i))
        if tag == "nsa" and i >= 3 and (i - 3) % 4 == 0:
            out.append(("nsa_cturn", (i - 3) // 4))
        if 2 <= i <= units + 1:
            out.append((f"{tag}_turn", i - 2))
        if i >= 3:
            out.append((f"{tag}_value", i - 3))
    return out


def product_list():
    m = ("mod", None)
    out = [m] * 4 + [("ssq", 0)]
    out += [("xr", j) for j in range(4)] + [("gr", j) for j in range(4)] + [m, m, ("gates", 0)]
    out += [(n, j) for j in range(4) for n in ("r", "i")] + [m, m]
    out += [("q", j) for j in range(4)] + [m, ("kcvc", 0), ("kcvc", 1), m, ("kskw", 0), ("kskw", 1), m]
    out += [("v", 0), ("v", 1), m]
    out += [("rope", j) for j in range(6)]
    out += [("cmp_h", 0), ("cmp_h", 1), ("cmp_o", 0), ("cmp_o", 1), ("sc", 0), ("sc", 1), ("sc", 2), ("sc", 3)]
    out += attention_order("nsa", 2 * HEADS)
    out += [("about", j) for j in range(4)] + [("ssq", 1), ("ssq", 2)]
    out += ffn_products(0, True, 12) + [("ssq", 3), ("ssq", 4)]
    for j in range(4):
        out += [("cg", j), ("scv", j), ("bg", j)] + ([m, m] if j else [])
    out += [("scout", 0), m, m, ("scout", 1), ("scout", 2), ("scout", 3), ("ssq", 5), ("ssq", 6)]
    out += ffn_products(1, True, 12) + [("ssq", 7)]
    out += [("poolp", 0), ("poolp", 1), ("qlat", 0), ("kvlat", 0), ("kvlat", 1), ("krope", 0)]
    out += [("qssq", 0), ("kvssq", 0), ("krot", 0)]
    out += [("qh", j) for j in range(4)] + [("knope", h) for h in range(MH)] + [("vm", j) for j in range(4)]
    out += [("qrot", j) for j in range(4)] + [("poold", 0), ("poold", 1), ("poolo", 0), ("poolo", 1)]
    out += attention_order("mla", 2 * MH)
    out += [("mixout", j) for j in range(4)] + [("mean", 0), ("ssq", 8)]
    out += ffn_products(2, False, 4) + [("mean", 1), ("ssq", 9)]
    out += [("sin", j) for j in range(3)] + [("filt", j) for j in range(8)]
    for j in range(4):
        out += [("hx1", j), ("hv", j), ("hx0", j)]
    out += [("wturn", j) for j in range(4)]
    for half in range(2):
        out += [("vspec", 4 * half + f) for f in range(4)]
        for i in range(2):
            out += [("kre", 2 * half + i), ("kim", 2 * half + i)]
        out += [("hconv", 2 * half + j) for j in range(2)]
    out += [("hyout", j) for j in range(4)] + [("mean", 2), ("ssq", 10), ("logits", 0)]
    out += [("tokens", j) for j in range(4)] + [("places", 0)]
    out += [("moeturn", j) for j in range(4)] + [("mean", 3), ("ssq", 11)]
    return out


def number_products():
    out, mods = {}, 0
    for n, (name, j) in enumerate(product_list()):
        if name == "mod":
            j, mods = mods, mods + 1
        assert (name, j) not in out, (name, j)
        out[name, j] = n
    assert mods == 48, mods
    return out


PRODUCT = number_products()


class Count:

    def __init__(self, sems, bank_free):
        self.sems, self.bank_free, self.counts = sems, bank_free, {}
        self.sem = self.value = None

    def up(self, name):
        self.counts[name] = self.counts.get(name, 0) + 1
        self.sem, self.value = self.sems.sem(name), self.counts[name]
        return self.sem

    def frees(self, name, j=0):
        n = PRODUCT[name, j]
        self.sem, self.value = self.bank_free[n % BANKS], n // BANKS + 1
        return self.sem


def made(name, j=0):
    return PRODUCT[name, j] + 1


class Shared:
    def __init__(self, nc, ctx):
        self.nc, self.ctx, self.sems = nc, ctx, {}

    def sem(self, name):
        if name not in self.sems:
            self.sems[name] = self.ctx.enter_context(self.nc.semaphore(name))
        return self.sems[name]

    def sb(self, name, shape, dt=F32):
        return self.ctx.enter_context(self.nc.sbuf_tensor(name, shape, dt))


def build(nc, stream, vecs_d, consts_d, tables_d, x_d, ctx_d, out_d):
    with ExitStack() as ctx:
        s = Shared(nc, ctx)
        ring = s.sb("ring", [P, RING, CH])
        vecs = s.sb("vecs_sb", [P, NCOL])
        consts = s.sb("consts_sb", [P, NCONST])
        arena = s.sb("arena", [P, 7 * 2048])
        R = s.sb("R", [P, 3072])
        TMP = s.sb("TMP", [P, 2048])
        stage = s.sb("stage", [P, 2, 2, 260])
        mod_acc = s.sb("mod_acc", [P, 2, 512])
        modv = s.sb("modv", [P, 4, 48])
        small = s.sb("small", [P, 512])
        idx = s.sb("idx", [P, 2, 8], U32)
        items = s.sb("items", [P, 5], mybir.dt.int32)
        s.psum = ctx.enter_context(nc.psum_tensor("psum", [P, BANKS, 512], F32))
        product_ready = s.sem("product_ready")
        bank_free = [s.sem(f"bank_free{i}") for i in range(BANKS)]
        block = ctx.enter_context(nc.Block())

        def bank_of(name, j=0):
            return s.psum[:, PRODUCT[name, j] % BANKS, :]

        def drained(name, j=0):
            n = PRODUCT[name, j]
            return bank_free[n % BANKS], n // BANKS + 1

        def region(i, n=1):
            return arena[:, 2048 * i:2048 * (i + n)]

        def feat(ap, t=T):
            return ap.rearrange("p (k t) -> p k t", t=t)

        def vec(name, i=0, n=1, rows=P):
            at = COL[name][0] + i
            return vecs[0:rows, at:at + n]

        def const(name, rows=P):
            at, w = CCOL[name]
            return consts[0:rows, at:at + w]

        X, H = feat(region(0)), feat(region(1))
        Y, SQ = feat(region(5)), feat(region(6))
        MIX = feat(region(2, 2))
        HID = feat(region(2, 3))
        XC, QRAW, QROT = feat(region(3)), feat(region(4)), feat(region(5))
        KCVC, KSKW = feat(R[:, 0:1024]), feat(R[:, 1024:2048])
        V = R[:, 2048:3072].rearrange("p (a n) -> p a n", a=2)
        t4 = TMP[:, :].rearrange("p (a n) -> p a n", a=4)
        eps_rms, eps_ln = small[:, 0:1], small[:, 1:2]
        c_act = small[:, 2:26]
        scale_a, shift_c = small[:, 26:34], small[:, 34:42]
        lru_c, lru_cn = small[:, 42:50], small[:, 50:58]
        gates = small[:, 64:160].rearrange("p (a h b) -> p a h b", a=2, b=3)
        cmp_bias = small[:, 160:162]
        hyp = small[:, 162:256]
        scale_x = small[:, 256:264]
        rstd = s.sb("rstd", [P, 512])
        c6 = region(6)
        cmp_hid = c6[:, 0:120].rearrange("p (b n) -> p b n", b=2)
        kcmp = c6[:, 128:188].rearrange("p (g n) -> p g n", n=NCMP)
        vcmp = c6[0:NCMP, 192:448].rearrange("p (g d) -> p g d", g=KVH)
        cx = c6[:, 512:992].rearrange("p (a h n) -> p a h n", a=2, n=NCMP)
        cmp_pt = R[0:NCMP, 0:1024].rearrange("p (a q t) -> p a q t", a=2, t=P)
        cstat = c6[:, 1024:1088].rearrange("p (a b h) -> p a b h", a=2, b=2)
        sstat = c6[:, 1100:1292].rearrange("p (u b c) -> p u b c", b=2, c=3)
        nsa_pt = region(4).rearrange("p (a n) -> p a n", a=4)[:, 0:2, :]
        mla_pt = R[:, 1024:2048].rearrange("p (a n) -> p a n", a=2)
        HC = region(1, 2).rearrange("p (k n) -> p k n", n=512)
        CTX = feat(region(3))
        POOLP = R[:, 0:1024].rearrange("p (a n) -> p a n", a=2)
        QL = feat(R[:, 1024:1536])
        KVL = R[:, 1536:2560].rearrange("p (a n) -> p a n", a=2)
        KM = region(1, 2).rearrange("p (h n) -> p h n", n=512)
        QM = feat(region(5))
        VM = region(4).rearrange("p (a n) -> p a n", n=512)
        MIXM = feat(region(3))
        POOLM = region(6).rearrange("p (a g t) -> p a g t", a=2, t=T)
        HF = region(2, 2).rearrange("p (a n) -> p a n", a=2)
        DECAY = region(4).rearrange("p (a n) -> p a n", a=2)
        WTOK = region(4).rearrange("p (a n) -> p a n", a=2)
        WF, X0 = feat(region(6)), feat(region(5))
        VS = region(1).rearrange("p (f n) -> p f n", n=512)
        FWD = R[:, 0:1024].rearrange("p (a f) -> p a f", a=2)
        BACK = R[:, 1024:2048].rearrange("p (a f) -> p a f", a=2)
        INV = feat(R[:, 2048:3072])
        ACC = region(2).rearrange("p (a n) -> p a n", a=2)
        moe_s = t4[:, 0:2, :]
        moe_h = t4[:, 2:4, :]
        moe_ht = region(3).rearrange("p (a n) -> p a n", a=4)[:, 0:2, :]
        TOK = region(4).rearrange("p (a n) -> p a n", a=2)
        XG = region(5)[:, 0:1024].rearrange("p (k t) -> p k t", t=P)
        YG = region(5)[:, 1024:2048]
        sel = region(6)[:, 0:256].rearrange("p (a n) -> p a n", a=2)
        sel_t = region(6)[:, 256:512]
        by_expert = small[:, 306:346].rearrange("p (c e) -> p c e", c=5)
        table = small[:, 346:406].rearrange("p (i c) -> p i c", c=5)
        chosen = small[:, 408:424].rearrange("p (a e) -> p a e", a=2)
        over_full, rank, hot = small[:, 424:432], small[:, 432:441], small[:, 442:450]
        picked = small[:, 450:490].rearrange("p (c e) -> p c e", c=5)
        head = small[:, 490:495]
        place_now = small[:, 496:498]
        lat_sq = region(6)
        kr_raw, kr_tmp = t4[:, 2, :], t4[:, 3, :]
        sines = TMP[0:64, 0:768].rearrange("p (j t) -> p j t", t=T)
        mstat = hyp[:, 16:64].rearrange("p (u c) -> p u c", c=3)
        modx = hyp[:, 64:80]
        comb_now = small[:, 304:306]
        COMB = hyp[:, 0:16].rearrange("p (a e) -> p a e", a=2)

        conv_users = {}

        def staged(name, j):
            return conv_users.setdefault((name, j), len(conv_users))

        for j in range(4):
            staged("xr", j)
        for j in range(11):
            staged("gate0", j)
        for j in range(4):
            staged("cv", j)
        for j in range(11):
            staged("gate1", j)
        for j in range(4):
            for n in ("hx1", "hv", "hx0"):
                staged(n, j)

        @block.sync
        def _(sp):
            n_chunks = stream.shape[0]
            for c in range(RING):
                sp.dma_start(ring[:, c, :], stream[c]).then_inc(s.sem(f"landed{c}"), 16)
            with sp.Fori(1, n_chunks // RING) as i:
                for c in range(RING):
                    sp.wait_ge(s.sem(f"used{c}"), i)
                    src = stream[bass.ds(i * RING + c, 1), :, :].rearrange("a p n -> (a p) n")
                    sp.dma_start(ring[:, c, :], src).then_inc(s.sem(f"landed{c}"), 16)
            i = n_chunks // RING
            for c in range(n_chunks % RING):
                sp.wait_ge(s.sem(f"used{c}"), i)
                sp.dma_start(ring[:, c, :], stream[i * RING + c]).then_inc(s.sem(f"landed{c}"), 16)
            sp.wait_ge(s.sem("items_ready"), 1)
            n_extra = sp.value_load(items[0:1, 1:2], min_val=0, max_val=EXTRA)
            with sp.If(n_extra > 0), sp.Fori(0, n_extra) as x:
                e = sp.value_load(items[0:1, bass.ds(x + 2, 1)], min_val=0, max_val=EXPERTS - 1)
                for k in range(3 * FEJ):
                    c = n_chunks + k
                    sp.wait_ge(s.sem(f"used{c % RING}"), (3 * FEJ // RING) * x + (c // RING))
                    src = stream[bass.ds(e * (3 * FEJ) + (MOE_BASE + k), 1), :, :].rearrange("a p n -> (a p) n")
                    sp.dma_start(ring[:, c % RING, :], src).then_inc(s.sem(f"landed{c % RING}"), 16)
            sp.wait_ge(s.sem("x2_ready"), 32)
            sp.dma_start(out_d, X).then_inc(s.sem("stored"), 16)
            sp.wait_ge(s.sem("stored"), 16)

        @block.tensor
        def _(eng):
            state = {"tile": 0, "product": 0}
            read = []
            ident, ones = const("ident"), const("ones")

            def mm(out, lhsT, rhs, start=True, stop=True, signal=None):
                ins = eng.matmul(out, lhsT, rhs, start=start, stop=stop)
                sign(ins, signal)

            def turn(out, in_, rows=P, signal=None):
                ins = eng.transpose(out, in_, ident[0:rows, 0:rows])
                sign(ins, signal)

            def sign(ins, signal):
                if signal is not None:
                    ins.then_inc(s.sem(signal), 1)
                elif read:
                    ins.then_inc(s.sem(f"used{read.pop(0) % RING}"), 1)

            def bank(name, j=0):
                n = PRODUCT[name, j]
                assert n == state["product"], (name, j, n, state["product"])
                state["product"] += 1
                if n >= BANKS:
                    eng.wait_ge(s.sem(f"bank_free{n % BANKS}"), n // BANKS)
                return s.psum[:, n % BANKS, :]

            def tiles(n=1, hold=False):
                t = state["tile"]
                c = P_CHUNKS[t // TILES]
                if t % TILES == 0:
                    eng.wait_ge(s.sem(f"landed{c % RING}"), 16 * (c // RING + 1))
                at = t % TILES
                assert at + n <= TILES
                state["tile"] += n
                if at + n == TILES and not hold:
                    read.append(c)
                return ring[:, c % RING, at * P:(at + n) * P]

            def release(pad=0):
                state["tile"] += pad
                assert state["tile"] % TILES == 0
                read.append(P_CHUNKS[state["tile"] // TILES - 1])

            def pair(name, j, src, kt=KT, ready=None):
                b = bank(name, j)
                for m in range(2):
                    for k in range(kt):
                        w = tiles()
                        if ready is not None and m == 0:
                            eng.wait_ge(s.sem(ready[0]), ready[1] + k)
                        mm(b[:, m * T:(m + 1) * T], w, src[:, k, :], k == 0, k == kt - 1,
                           "product_ready" if m == 1 and k == kt - 1 else None)

            mods = [0]

            def mod_sum():
                d = mods[0]
                mods[0] += 1
                c = D_CHUNKS[d]
                b = bank("mod", d)
                eng.wait_ge(s.sem(f"used{c % RING}"), c // RING + 1)
                n = 8 if 24 <= d < 28 else 4
                if n == 8:
                    eng.wait_ge(s.sem("ctx_acc"), d - 23)
                for q in range(n):
                    acc = mod_acc[:, d % 2, :] if q < 4 else R[:, 512 * (d % 2):512 * (d % 2) + 512]
                    mm(b[:, q:q + 1], acc[:, (q % 4) * P:(q % 4 + 1) * P], ones[:, 0:1],
                       signal="product_ready" if q == n - 1 else None)

            def col_sums(name, j, src, ready, base, kt=KT, width=T):
                b = bank(name, j)
                for k in range(kt):
                    eng.wait_ge(s.sem(ready), base + k // 2 + 1)
                    mm(b[:, 0:width], ones, src[:, k, :], k == 0, k == kt - 1,
                       "product_ready" if k == kt - 1 else None)

            def pair_down(tag, j):
                b = bank(f"down{tag}", j)
                for m in range(2):
                    for k in range(FT):
                        w = tiles()
                        if j == 0 and m == 0 and k % 2 == 0:
                            eng.wait_ge(*drained(f"up{tag}", k // 2))
                        mm(b[:, m * T:(m + 1) * T], w, HID[:, k, :], k == 0, k == FT - 1,
                           "product_ready" if m == 1 and k == FT - 1 else None)

            def feed_forward(tag, mods_here, h_base):
                for j in range(FT // 2):
                    pair(f"gate{tag}", j, H, ready=("h_ready", h_base + 1) if j == 0 else None)
                    pair(f"up{tag}", j, H)
                    if 0 <= j - 1 < mods_here:
                        mod_sum()
                for j in range(4):
                    pair_down(tag, j)
                    if (j == 0 and mods_here >= 11) or (j == 1 and mods_here == 12):
                        mod_sum()

            def gather(i):
                eng.wait_ge(s.sem("sel_made"), i + 1)
                for h in range(2):
                    for k in range(4):
                        for a in range(2):
                            m = 4 * h + k
                            mm_plain(s.psum[:, 6 + h, k * P:(k + 1) * P], TOK[:, a, m * P:(m + 1) * P],
                                     sel[:, a, :], a == 0, a == 1, "moe_gathered" if k == 3 and a else None)

            def expert(e):
                def landed(k):
                    c = MOE_BASE + k
                    eng.wait_ge(s.sem(f"landed{c % RING}"), 3 * 16 * e + 16 * (c // RING + 1))
                    return ring[:, c % RING, :], f"used{c % RING}"

                for q in range(FEJ + 2):
                    if q < FEJ:
                        if q == 0:
                            eng.wait_ge(s.sem("moe_acc"), 4 * e + 2)
                        elif q == 1:
                            eng.wait_ge(s.sem("moe_acc"), 4 * e + 4)
                        else:
                            eng.wait_ge(s.sem("moe_turned"), FEJ * e + q - 1)
                        for i in range(2):
                            w, used = landed(expert_chunk(i, q))
                            for k in range(KT):
                                if q == 0 and i == 0 and k % 4 == 0:
                                    eng.wait_ge(s.sem("moe_xg"), 2 * e + k // 4 + 1)
                                last = k == KT - 1
                                mm_plain(s.psum[:, 2 * (q % 2) + i, :], XG[:, k, :],
                                         w[:, k * 512:(k + 1) * 512], k == 0, last,
                                         ("moe_gu" if i else used) if last else None)
                    if q == 0:
                        eng.transpose(s.psum[:, 6, 0:P], sel[:, 0, :], ident).then_inc(s.sem(used), 1)
                        eng.transpose(s.psum[:, 6, P:2 * P], sel[:, 1, :], ident).then_inc(s.sem("sel_turned"), 1)
                    if 1 <= q <= FEJ:
                        u = q - 1
                        eng.wait_ge(s.sem("moe_h"), FEJ * e + u + 1)
                        for f in range(4):
                            ins = eng.transpose(s.psum[:, 2 * (u % 2), f * P:(f + 1) * P],
                                                moe_h[:, u % 2, f * P:(f + 1) * P], ident)
                            if f == 0 and q < FEJ:
                                ins.then_inc(s.sem(used), 1)
                            if f == 3:
                                ins.then_inc(s.sem("moe_t"), 1)
                    if q >= 2:
                        u = q - 2
                        w, used_down = landed(expert_chunk(2, u))
                        eng.wait_ge(s.sem("moe_turned"), FEJ * e + u + 1)
                        for f in range(4):
                            for n in range(2):
                                mm_plain(s.psum[:, 4 + n, :], moe_ht[:, u % 2, f * P:(f + 1) * P],
                                         w[:, f * D + n * 512:f * D + (n + 1) * 512], u == 0 and f == 0,
                                         u == FEJ - 1 and f == 3, used_down if f == 3 and n else None)
                eng.wait_ge(s.sem("sel_t_ready"), e + 1)
                gather(e + 1)
                for a in range(2):
                    for n in range(2):
                        if a == 0:
                            eng.wait_ge(s.sem("moe_y"), 2 * e + n + 1)
                        mm_plain(s.psum[:, 2 * a + n, :], sel_t[:, a * P:(a + 1) * P],
                                 YG[:, n * 512:(n + 1) * 512], True, True, "moe_out")

            def mm_plain(out, lhsT, rhs, start, stop, signal):
                ins = eng.matmul(out, lhsT, rhs, start=start, stop=stop)
                if signal:
                    ins.then_inc(s.sem(signal), 1)

            eng.wait_ge(s.sem("consts_loaded"), 48)
            for _ in range(4):
                mod_sum()
            col_sums("ssq", 0, SQ, "sq_ready", 0)
            for j in range(4):
                pair("xr", j, H, ready=("h_ready", 1) if j == 0 else None)
            for j in range(4):
                pair("gr", j, H)
            mod_sum()
            mod_sum()
            wg = tiles(3)
            b = bank("gates")
            for a in range(2):
                for k in range(KT):
                    mm(b[:, a * 48:(a + 1) * 48], H[:, k, a * P:(a + 1) * P], wg[:, k * 48:(k + 1) * 48],
                       k == 0, k == KT - 1, "product_ready" if a == 1 and k == KT - 1 else None)
            w_r, w_i = tiles(8), tiles(8)
            for j in range(4):
                eng.wait_ge(s.sem("conv_done"), j + 1)
                for name, w in (("r", w_r), ("i", w_i)):
                    b = bank(name, j)
                    for m in range(2):
                        k = 2 * j + m
                        mm(b[:, m * T:(m + 1) * T], w[:, k * P:(k + 1) * P], XC[:, k, :],
                           signal="product_ready" if m else None)
            release(TILES - 19)
            mod_sum()
            mod_sum()
            for j in range(4):
                pair("q", j, H)
            mod_sum()
            for j in range(2):
                pair("kcvc", j, H)
            mod_sum()
            for j in range(2):
                pair("kskw", j, H)
            mod_sum()
            wv = tiles(32, hold=True)
            for a in range(2):
                b = bank("v", a)
                for k in range(KT):
                    mm(b, H[:, k, a * P:(a + 1) * P], wv[:, k * 512:(k + 1) * 512], k == 0, k == KT - 1,
                       "product_ready" if k == KT - 1 else None)
            release()
            mod_sum()
            for j in range(6):
                if j < 4:
                    eng.wait_ge(*drained("q", j))
                else:
                    eng.wait_ge(*drained("kskw", j - 4))
                src = QRAW[:, 2 * j:2 * j + 2, :] if j < 4 else KSKW[:, 2 * (j - 4):2 * (j - 4) + 2, :]
                mm(bank("rope", j), const("rope_r"), src, signal="product_ready")
            eng.wait_ge(*drained("kcvc", 1))
            w1 = tiles(32, hold=True)
            for i in range(2):
                rows = slice(64 * i, 64 * i + 64)
                b = bank("cmp_h", i)
                for l in range(CMPB):
                    mm(b[:, 0:60].rearrange("p (g n) -> p g n", n=NCMP), w1[rows, l * P:(l + 1) * P],
                       KCVC[rows, :, l:l + CMPS * (NCMP - 1) + 1:CMPS], l == 0, l == CMPB - 1)
                for l in range(CMPB):
                    mm(b[:, 64:65], w1[rows, l * P:(l + 1) * P], vec("pe_t", l)[rows, :], l == 0, l == CMPB - 1,
                       "product_ready" if l == CMPB - 1 else None)
            release()
            eng.wait_ge(*drained("cmp_h", 0))
            mm(bank("cmp_o", 0)[:, 0:60], vec("wk2", 0, P), cmp_hid[:, 0, :], signal="product_ready")
            eng.wait_ge(*drained("cmp_h", 1))
            b = bank("cmp_o", 1)
            for g in range(KVH):
                mm(b[0:NCMP, g * HD:(g + 1) * HD], cmp_hid[:, 1, g * NCMP:(g + 1) * NCMP], vec("wv2", 0, HD),
                   signal="product_ready" if g == KVH - 1 else None)
            eng.wait_ge(*drained("cmp_o", 0))
            for a in range(2):
                for half in range(2):
                    b = bank("sc", 2 * a + half)
                    rows = slice(64 * half, 64 * half + 64)
                    for m in range(8):
                        mm(b[:, m * NCMP:(m + 1) * NCMP], QRAW[rows, m, a * P:(a + 1) * P],
                           kcmp[rows, 2 * (m // 4) + half, :], signal="product_ready" if m == 7 else None)

            def nsa_unit(u):
                hh, a = u // 2, u % 2
                m, half = hh // 2, hh % 2
                g, r = 2 * (m // 4) + half, m % 4
                return m, half, g, 4 * g + r, a

            for name, u in attention_order("nsa", 2 * HEADS):
                b = bank(name, u)
                if name == "nsa_cturn":
                    if u == 0:
                        eng.wait_ge(s.sem("cmp_probs"), 2)
                    for q in range(4):
                        _, _, _, h, a = nsa_unit(4 * u + q)
                        turn(b[0:NCMP, q * P:(q + 1) * P], cx[:, a, h, :], signal="product_ready" if q == 3 else None)
                    continue
                m, half, g, h, a = nsa_unit(u)
                rows = slice(64 * half, 64 * half + 64)
                nk = (a + 1) * P
                if name == "nsa_scores":
                    if u == 0:
                        eng.wait_ge(s.sem("roped"), 6)
                    for w in range(2):
                        mm(b[:, w * T:w * T + nk], QROT[rows, m, a * P:(a + 1) * P],
                           KSKW[rows, 2 * w + m // 4, 0:nk], signal="product_ready" if w else None)
                elif name == "nsa_turn":
                    eng.wait_ge(s.sem("probs"), u + 1)
                    x = t4[:, u % 4, :]
                    n = 0
                    for w in range(2):
                        for kt in range(a + 1):
                            last = n == 2 * a + 1
                            turn(b[:, n * P:(n + 1) * P], x[:, w * T + kt * P:w * T + (kt + 1) * P],
                                 signal="product_ready" if last else None)
                            n += 1
                else:
                    eng.wait_ge(*drained("nsa_turn", u))
                    pt = nsa_pt[:, u % 2, :]
                    n = 0
                    for w in range(2):
                        for kt in range(a + 1):
                            mm(b[0:HD, 0:P], V[:, kt, w * T + g * HD:w * T + (g + 1) * HD],
                               pt[:, n * P:(n + 1) * P], n == 0, False)
                            n += 1
                    if u % 4 == 0:
                        eng.wait_ge(*drained("nsa_cturn", u // 4))
                    mm(b[0:HD, 0:P], vcmp[:, g, :], cmp_pt[:, u // 4 % 2, u % 4, :], False, True, "product_ready")
            eng.wait_ge(s.sem("rnn_mixed"), 4)
            eng.wait_ge(*drained("nsa_value", 2 * HEADS - 1))
            for j in range(4):
                pair("about", j, MIX, 16)
            col_sums("ssq", 1, SQ, "sq_ready", 4)
            col_sums("ssq", 2, SQ, "sq_ready", 8)
            feed_forward(0, 12, 8)
            col_sums("ssq", 3, SQ, "sq_ready", 12)
            col_sums("ssq", 4, SQ, "sq_ready", 16)
            for j in range(4):
                pair("cg", j, H, ready=("h_ready", 17) if j == 0 else None)
                pair("scv", j, H)
                pair("bg", j, H)
                if j:
                    mod_sum()
                    mod_sum()
            for j in range(4):
                if j == 0:
                    eng.wait_ge(*drained("bg", 3))
                pair("scout", j, MIX)
                if j == 0:
                    mod_sum()
                    mod_sum()
            col_sums("ssq", 5, SQ, "sq_ready", 20)
            col_sums("ssq", 6, SQ, "sq_ready", 24)
            feed_forward(1, 12, 24)
            col_sums("ssq", 7, SQ, "sq_ready", 28)

            wp = tiles(32, hold=True)
            for a in range(2):
                b = bank("poolp", a)
                for k in range(KT):
                    eng.wait_ge(s.sem("h_ready"), 33 + k)
                    mm(b, HC[:, k, a * P:(a + 1) * P], wp[:, k * 512:(k + 1) * 512], k == 0, k == KT - 1,
                       "product_ready" if k == KT - 1 else None)
            release()
            pair("qlat", 0, HC[:, :, 0:T])
            eng.wait_ge(s.sem("h_ready"), 48)
            for m in range(2):
                b = bank("kvlat", m)
                for k in range(KT):
                    mm(b, tiles(), HC[:, k, :], k == 0, k == KT - 1, "product_ready" if k == KT - 1 else None)
            wkr = tiles(2)
            b = bank("krope")
            for k in range(KT):
                mm(b[0:ROPE, :], wkr[:, k * ROPE:(k + 1) * ROPE], HC[:, k, :], k == 0, k == KT - 1,
                   "product_ready" if k == KT - 1 else None)
            b = bank("qssq")
            eng.wait_ge(s.sem("lat_sq"), 1)
            for k in range(2):
                mm(b[:, 0:T], ones, lat_sq[:, k * T:(k + 1) * T], k == 0, k == 1, "product_ready" if k else None)
            b = bank("kvssq")
            eng.wait_ge(s.sem("lat_sq"), 3)
            for k in range(2):
                mm(b, ones, lat_sq[:, 512 + k * 512:1024 + k * 512], k == 0, k == 1, "product_ready" if k else None)
            eng.wait_ge(*drained("krope"))
            mm(bank("krot")[0:ROPE, 0:T], const("kr_r", ROPE), kr_raw[0:ROPE, 0:T], signal="product_ready")
            wqu, wkn, wvm = tiles(12), tiles(8), tiles(8)
            eng.wait_ge(s.sem("q_normed"), 1)
            for j in range(4):
                b = bank("qh", j)
                for i in range(2):
                    for k in range(2):
                        at = ((2 * j + i) * 2 + k) * 96
                        mm(b[0:96, i * T:(i + 1) * T], wqu[:, at:at + 96], QL[:, k, :], k == 0, k == 1,
                           "product_ready" if i and k else None)
            eng.wait_ge(s.sem("kv_normed"), 1)
            for h in range(MH):
                b = bank("knope", h)
                for k in range(2):
                    at = (2 * h + k) * NOPE
                    mm(b[0:NOPE, :], wkn[:, at:at + NOPE], KVL[:, k, :], k == 0, k == 1, "product_ready" if k else None)
            for kt in range(4):
                b = bank("vm", kt)
                for k in range(2):
                    mm(b, KVL[:, k, kt * P:(kt + 1) * P], wvm[:, k * 512:(k + 1) * 512], k == 0, k == 1,
                       "product_ready" if k else None)
            for j in range(4):
                eng.wait_ge(*drained("qh", j))
                mm(bank("qrot", j)[0:96, :], const("mla_r", 96), QM[0:96, 2 * j:2 * j + 2, :], signal="product_ready")
            eng.wait_ge(*drained("poolp", 1))
            eng.wait_ge(s.sem("pool_table"), 16)
            for j in range(2):
                b = bank("poold", j)
                for i in range(2):
                    for a in range(2):
                        g = 2 * j + i
                        mm(b[:, i * T:(i + 1) * T], POOLP[:, a, g * P:(g + 1) * P], POOLM[:, a, g, :], a == 0, a == 1,
                           "product_ready" if i and a else None)
            for j in range(2):
                b = bank("poolo", j)
                eng.wait_ge(*drained("poold", j))
                for i in range(2):
                    mm(b[:, i * T:(i + 1) * T], tiles(), t4[:, j, i * T:(i + 1) * T],
                       signal="product_ready" if i else None)
            state["tile"] += 14
            for name, u in attention_order("mla", 2 * MH):
                h, a = u // 2, u % 2
                b = bank(name, u)
                if name == "mla_scores":
                    if u == 0:
                        eng.wait_ge(s.sem("k_filled"), MH)
                        eng.wait_ge(*drained("knope", MH - 1))
                        eng.wait_ge(*drained("vm", 3))
                        eng.wait_ge(s.sem("q_roped"), 4)
                    mm(b, QM[0:96, h, a * P:(a + 1) * P], KM[0:96, h, :], signal="product_ready")
                elif name == "mla_turn":
                    eng.wait_ge(s.sem("mla_probs"), u + 1)
                    for kt in range(4):
                        turn(b[:, kt * P:(kt + 1) * P], t4[:, u % 4, kt * P:(kt + 1) * P],
                             signal="product_ready" if kt == 3 else None)
                else:
                    eng.wait_ge(*drained("mla_turn", u))
                    for kt in range(4):
                        mm(b[0:VH, 0:P], VM[:, kt, h * VH:(h + 1) * VH], mla_pt[:, u % 2, kt * P:(kt + 1) * P],
                           kt == 0, kt == 3, "product_ready" if kt == 3 else None)
            eng.wait_ge(*drained("poolo", 1))
            eng.wait_ge(*drained("mla_value", 2 * MH - 1))
            for j in range(4):
                pair("mixout", j, MIXM)
            col_sums("mean", 0, X, "z_ready", 0)
            col_sums("ssq", 8, SQ, "sq_ready", 32)
            feed_forward(2, 4, 48)
            col_sums("mean", 1, X, "z_ready", 4)
            col_sums("ssq", 9, SQ, "sq_ready", 36)

            for j in range(3):
                rows = 33 if j == 0 else 64
                rhs = vec("z_t", 0, T, 33) if j == 0 else sines[0:64, j - 1, :]
                if j:
                    eng.wait_ge(s.sem("sine"), j)
                mm(bank("sin", j)[0:64, 0:T], vec("fw", 64 * j, 64, rows), rhs, signal="product_ready")
            wf = tiles(16)
            eng.wait_ge(s.sem("sine"), 3)
            for j in range(8):
                a, n = j // 4, j % 4
                mm(bank("filt", j), sines[0:64, 2, a * P:(a + 1) * P], wf[0:64, n * 512:(n + 1) * 512],
                   signal="product_ready")
            for j in range(4):
                pair("hx1", j, H, ready=("h_ready", 57) if j == 0 else None)
                pair("hv", j, H)
                pair("hx0", j, H)
            for j in range(4):
                b = bank("wturn", j)
                eng.wait_ge(s.sem("w_ready"), j + 1)
                for i in range(4):
                    turn(b[:, i * P:(i + 1) * P], WF[:, 2 * j + i // 2, (i % 2) * P:(i % 2 + 1) * P],
                         signal="product_ready" if i == 3 else None)
            eng.wait_ge(s.sem("dft_tables"), 16)
            eng.wait_ge(*drained("wturn", 3))
            for half in range(2):
                for f in range(4):
                    b = bank("vspec", 4 * half + f)
                    for a in range(2):
                        mm(b, FWD[:, a, f * P:(f + 1) * P], WTOK[:, a, half * 512:(half + 1) * 512], a == 0, a == 1,
                           "product_ready" if a else None)
                eng.wait_ge(*drained("filt", 7))
                for i in range(2):
                    for f, name in ((i, "kre"), (2 + i, "kim")):
                        b = bank(name, 2 * half + i)
                        for a in range(2):
                            mm(b, FWD[:, a, f * P:(f + 1) * P], HF[:, a, half * 512:(half + 1) * 512], a == 0, False)
                            mm(b, BACK[:, a, f * P:(f + 1) * P], HF[:, a, D + half * 512:D + (half + 1) * 512],
                               False, a == 1, "product_ready" if a else None)
                eng.wait_ge(s.sem("spectrum"), 2 * half + 2)
                for j in range(2):
                    b = bank("hconv", 2 * half + j)
                    for i in range(2):
                        for f in range(4):
                            m = 2 * j + i
                            mm(b[:, i * T:(i + 1) * T], VS[:, f, m * P:(m + 1) * P], INV[:, f, :], f == 0, f == 3,
                               "product_ready" if i and f == 3 else None)
            eng.wait_ge(s.sem("hy_mixed"), 4)
            for j in range(4):
                pair("hyout", j, WF)
            col_sums("mean", 2, X, "z_ready", 8)
            col_sums("ssq", 10, SQ, "sq_ready", 40)
            release(TILES - state["tile"] % TILES)
            b = bank("logits")
            for a in range(2):
                for k in range(KT):
                    eng.wait_ge(s.sem("h_ready"), 65 + k)
                    mm(b[:, a * EXPERTS:(a + 1) * EXPERTS], H[:, k, a * P:(a + 1) * P],
                       vec("router", k * EXPERTS, EXPERTS), k == 0, k == KT - 1,
                       "product_ready" if a and k == KT - 1 else None)
            for j in range(4):
                b = bank("tokens", j)
                for i in range(4):
                    m, a = 2 * j + i // 2, i % 2
                    turn(b[:, i * P:(i + 1) * P], H[:, m, a * P:(a + 1) * P],
                         signal="product_ready" if i == 3 else None)
            b = bank("places")
            eng.wait_ge(s.sem("chosen_ready"), 1)
            mm(b[:, 0:8], const("earlier"), chosen[:, 0, :])
            mm(b[:, 8:16], ones, chosen[:, 0, :], True, False)
            mm(b[:, 8:16], const("earlier"), chosen[:, 1, :], False, True)
            mm(b[:, 16:24], ones, chosen[:, 0, :], True, False)
            mm(b[:, 16:24], ones, chosen[:, 1, :], False, True, "product_ready")
            for n in range(PRODUCT["places", 0] - BANKS + 1, PRODUCT["places", 0] + 1):
                eng.wait_ge(s.sem(f"bank_free{n % BANKS}"), n // BANKS + 1)
            eng.wait_ge(s.sem("items_ready"), 1)
            n_items = eng.value_load(items[0:1, 0:1], min_val=EXPERTS, max_val=EXPERTS + EXTRA)
            gather(0)
            with eng.Fori(0, n_items) as e:
                expert(e)
            eng.wait_ge(s.sem("moe_xg"), 2 * n_items + 2)
            for j in range(4):
                b = bank("moeturn", j)
                if j == 0:
                    eng.wait_ge(s.sem("moe_acc"), 4 * n_items + 4)
                for i in range(4):
                    m, a = 2 * j + i // 2, i % 2
                    turn(b[:, i * P:(i + 1) * P], ACC[:, a, m * P:(m + 1) * P],
                         signal="product_ready" if i == 3 else None)
            col_sums("mean", 3, X, "z_ready", 12)
            col_sums("ssq", 11, SQ, "sq_ready", 44)
            assert state["product"] == len(PRODUCT), state["product"]

        @block.scalar
        def _(eng):
            own = Count(s, bank_free)
            eng.dma_start(vecs[:, :], vecs_d).then_inc(s.sem("consts_loaded"), 16)
            eng.dma_start(consts[:, :], consts_d).then_inc(s.sem("consts_loaded"), 16)
            eng.dma_start(X, x_d).then_inc(s.sem("consts_loaded"), 16)
            eng.wait_ge(s.sem("consts_loaded"), 48)
            eng.wait_ge(s.sem("cleared"), 1)

            def f(out, in_, func=ACT.Copy, **kw):
                return eng.activation(out, in_, func, **kw)

            def halves(b):
                return feat(b)

            def pre_norm(n, layer, half, x_stage):
                if x_stage:
                    eng.wait_ge(s.sem("x1_ready"), x_stage)
                for j in range(4):
                    f(SQ[:, 2 * j:2 * j + 2, :], X[:, 2 * j:2 * j + 2, :], ACT.Square).then_inc(own.up("sq_ready"), 1)
                eng.wait_ge(product_ready, made("ssq", 2 * n))
                b = bank_of("ssq", 2 * n)
                f(rstd[:, 0:T], b[:, 0:T], ACT.Sqrt, scale=1.0 / D, bias=eps_rms).then_inc(own.frees("ssq", 2 * n), 1)
                for k in range(KT):
                    eng.wait_ge(s.sem("normed"), 8 * n + k + 1)
                    f(H[:, k, :], H[:, k, :], ACT.Identity, scale=scale_a[:, k:k + 1],
                          bias=modv[:, layer, 24 * half + k:24 * half + k + 1]).then_inc(own.up("h_ready"), 1)

            def post_norm(n, name):
                for j in range(4):
                    eng.wait_ge(product_ready, made(name, j))
                    b = bank_of(name, j)
                    f(SQ[:, 2 * j:2 * j + 2, :], halves(b), ACT.Square).then_inc(own.up("sq_ready"), 1)
                    f(Y[:, 2 * j:2 * j + 2, :], halves(b)).then_inc(own.frees(name, j), 1)
                eng.wait_ge(product_ready, made("ssq", n))
                b = bank_of("ssq", n)
                f(rstd[:, 0:T], b[:, 0:T], ACT.Sqrt, scale=1.0 / D, bias=eps_rms).then_inc(own.frees("ssq", n), 1)

            def stage_in(name, j):
                n = staged(name, j)
                eng.wait_ge(product_ready, made(name, j))
                b = bank_of(name, j)
                if n >= 2:
                    eng.wait_ge(s.sem("conv_done"), n - 1)
                f(stage[:, n % 2, :, 3:259], halves(b)).then_inc(own.frees(name, j), 1)

            def feed_forward(tag):
                for j in range(FT // 2):
                    if tag < 2:
                        stage_in(f"gate{tag}", j)
                        eng.wait_ge(s.sem("conv_done"), staged(f"gate{tag}", j) + 1)
                        if j >= 2:
                            eng.wait_ge(*drained(f"up{tag}", j - 2))
                        f(t4[:, 2 + j % 2, :], t4[:, j % 2, :], ACT.Silu).then_inc(own.up("silu"), 1)
                    else:
                        eng.wait_ge(product_ready, made(f"gate{tag}", j))
                        b = bank_of(f"gate{tag}", j)
                        if j >= 2:
                            eng.wait_ge(*drained(f"up{tag}", j - 2))
                        f(t4[:, 2 + j % 2, :], b, ACT.Silu).then_inc(own.frees(f"gate{tag}", j), 1)

            def layer_norm(n, name, layer, gate_at):
                eng.wait_ge(s.sem("mod_done"), 24 + 12 * (layer - 2) + (gate_at + 8) // 4)
                for j in range(4):
                    eng.wait_ge(product_ready, made(name, j))
                    b = bank_of(name, j)
                    for i in range(2):
                        k = 2 * j + i
                        ins = f(Y[:, k, :], b[:, i * T:(i + 1) * T], ACT.Copy,
                                scale=modv[:, layer, gate_at + k:gate_at + k + 1])
                    ins.then_inc(own.frees(name, j), 1)
                for j in range(4):
                    eng.wait_ge(s.sem("centred"), 4 * n + j + 1)
                    f(SQ[:, 2 * j:2 * j + 2, :], X[:, 2 * j:2 * j + 2, :], ACT.Square).then_inc(own.up("sq_ready"), 1)
                eng.wait_ge(product_ready, made("ssq", 8 + n))
                b = bank_of("ssq", 8 + n)
                f(rstd[:, 0:T], b[:, 0:T], ACT.Sqrt, scale=1.0 / D, bias=eps_ln).then_inc(own.frees("ssq", 8 + n), 1)
                for k in range(KT):
                    eng.wait_ge(s.sem("ln_scaled"), 4 * n + k // 2 + 1)
                    f(X[:, k, :], X[:, k, :], ACT.Identity, scale=vec("ln_g", 8 * n + k),
                          bias=vec("ln_b", 8 * n + k)).then_inc(own.up("x2_ready"), 1)

            def modulate(dst, src, coef, scale, shift):
                eng.wait_ge(s.sem("coef"), coef)
                eng.wait_ge(own.sem, own.value)
                for k in range(KT):
                    f(dst[:, k, :], src[:, k, :], ACT.Identity, scale=scale[:, k:k + 1],
                          bias=shift[:, k:k + 1]).then_inc(own.up("h_ready"), 1)

            f(c_act, vec("c", 0, 24), ACT.Silu).then_inc(own.up("c_act"), 1)
            eng.wait_ge(s.sem("lam_abs"), 1)
            f(lru_cn, lru_c, ACT.Exp, scale=-1.0).then_inc(own.up("lam_exp"), 1)
            pre_norm(0, 0, 0, 0)
            for j in range(4):
                stage_in("xr", j)
            for j in range(4):
                eng.wait_ge(product_ready, made("gr", j))
                b = bank_of("gr", j)
                f(MIX[:, 2 * j:2 * j + 2, :], halves(b), ACT.Gelu_apprx_tanh).then_inc(own.frees("gr", j), 1)
            eng.wait_ge(product_ready, made("gates"))
            b = bank_of("gates")
            f(small[:, 64:160], b[:, 0:96], ACT.Sigmoid).then_inc(own.frees("gates"), 1)
            lru_r, lru_i, lru_a = feat(region(5)), feat(region(6)), feat(region(4))
            for j in range(4):
                for name, dst, bias in (("r", lru_r, "lru_b_r"), ("i", lru_i, "lru_b_i")):
                    eng.wait_ge(product_ready, made(name, j))
                    b = bank_of(name, j)
                    for i in range(2):
                        ins = f(dst[:, 2 * j + i, :], b[:, i * T:(i + 1) * T], ACT.Sigmoid, bias=vec(bias, 2 * j + i))
                    ins.then_inc(own.frees(name, j), 1)
            eng.wait_ge(s.sem("lru_coef"), 1)
            eng.wait_ge(own.sem, own.value)
            for k in range(KT):
                f(lru_a[:, k, :], lru_r[:, k, :], ACT.Exp, scale=lru_c[:, k:k + 1]).then_inc(own.up("act_step"), 1)
                f(lru_r[:, k, :], lru_r[:, k, :], ACT.Tanh, scale=lru_cn[:, k:k + 1]).then_inc(own.up("lru_t"), 1)
            for j in range(4):
                eng.wait_ge(s.sem("lru_w"), j + 1)
                f(lru_r[:, 2 * j:2 * j + 2, :], lru_r[:, 2 * j:2 * j + 2, :], ACT.Sqrt, scale=2.0).then_inc(own.up("lru_s"), 1)
            eng.wait_ge(s.sem("rnn_mixed"), 4)
            for name, n, dst in (("q", 4, QRAW), ("kcvc", 2, KCVC), ("kskw", 2, KSKW)):
                for j in range(n):
                    eng.wait_ge(product_ready, made(name, j))
                    b = bank_of(name, j)
                    f(dst[:, 2 * j:2 * j + 2, :], halves(b)).then_inc(own.frees(name, j), 1)
            for a in range(2):
                eng.wait_ge(product_ready, made("v", a))
                b = bank_of("v", a)
                f(V[:, a, :], b).then_inc(own.frees("v", a), 1)
            for i in range(2):
                eng.wait_ge(s.sem("cmp_bias"), i + 1)
                eng.wait_ge(product_ready, made("cmp_h", i))
                b = bank_of("cmp_h", i)
                f(cmp_hid[:, i, :], b[:, 0:60], ACT.Gelu_apprx_tanh, bias=cmp_bias[:, i:i + 1]).then_inc(own.frees("cmp_h", i), 1)
            eng.wait_ge(product_ready, made("cmp_o", 0))
            b = bank_of("cmp_o", 0)
            f(c6[:, 128:188], b[:, 0:60]).then_inc(own.frees("cmp_o", 0), 1)
            eng.wait_ge(product_ready, made("cmp_o", 1))
            b = bank_of("cmp_o", 1)
            f(c6[0:NCMP, 192:448], b[0:NCMP, 0:256]).then_inc(own.frees("cmp_o", 1), 1)
            for a in range(2):
                eng.wait_ge(s.sem("cmp_shifted"), a + 1)
                f(cx[:, a], cx[:, a], ACT.Exp, scale=HD ** -0.5).then_inc(own.up("cmp_exp"), 1)
            for name, u in attention_order("nsa", 2 * HEADS):
                if name == "nsa_scores":
                    a = u % 2
                    eng.wait_ge(s.sem("shifted"), u + 1)
                    for w in range(2):
                        x = t4[:, u % 4, w * T:w * T + (a + 1) * P]
                        f(x, x, ACT.Exp, scale=HD ** -0.5, bias=sstat[:, u, w, 0:1],
                              accum_out=sstat[:, u, w, 1:2]).then_inc(own.up("exps"), 1)
                elif name == "nsa_cturn":
                    eng.wait_ge(product_ready, made(name, u))
                    b = bank_of(name, u)
                    f(R[0:NCMP, 512 * (u % 2):512 * (u % 2) + 512], b[0:NCMP, :]).then_inc(own.frees(name, u), 1)
                elif name == "nsa_turn":
                    eng.wait_ge(product_ready, made(name, u))
                    b = bank_of(name, u)
                    n = 2 * (u % 2 + 1) * P
                    f(nsa_pt[:, u % 2, 0:n], b[:, 0:n]).then_inc(own.frees(name, u), 1)
                else:
                    hh, a = u // 2, u % 2
                    h = 4 * (2 * (hh // 2 // 4) + hh % 2) + hh // 2 % 4
                    eng.wait_ge(product_ready, made(name, u))
                    b = bank_of(name, u)
                    rows = slice(64 * (h % 2), 64 * (h % 2) + 64)
                    f(MIX[rows, 8 + h // 2, a * P:(a + 1) * P], b[0:HD, 0:P]).then_inc(own.frees(name, u), 1)
            post_norm(1, "about")
            pre_norm(1, 0, 1, 1)
            feed_forward(0)
            post_norm(3, "down0")
            pre_norm(2, 1, 0, 2)
            for j in range(4):
                eng.wait_ge(product_ready, made("cg", j))
                b = bank_of("cg", j)
                if j >= 2:
                    eng.wait_ge(*drained("scv", j - 2))
                f(t4[:, j % 2, :], b).then_inc(own.frees("cg", j), 1)
            post_norm(5, "scout")
            pre_norm(3, 1, 1, 3)
            feed_forward(1)
            eng.wait_ge(product_ready, made("down1", 3))
            eng.dma_start(CTX, ctx_d).then_inc(s.sem("ctx_loaded"), 16)
            post_norm(7, "down1")

            eng.wait_ge(s.sem("x1_ready"), 4)
            modulate(HC[:, :, 0:T], X, 1, scale_a, modv[:, 2, 0:8])
            eng.wait_ge(s.sem("ctx_loaded"), 16)
            modulate(HC[:, :, T:2 * T], CTX, 1, scale_x, modx[:, 0:8])
            for a in range(2):
                eng.wait_ge(product_ready, made("poolp", a))
                b = bank_of("poolp", a)
                f(POOLP[:, a, :], b).then_inc(own.frees("poolp", a), 1)
            eng.wait_ge(product_ready, made("qlat", 0))
            b = bank_of("qlat", 0)
            f(lat_sq[:, 0:512], b, ACT.Square).then_inc(own.up("lat_sq"), 1)
            f(R[:, 1024:1536], b).then_inc(own.frees("qlat", 0), 1)
            for m in range(2):
                eng.wait_ge(product_ready, made("kvlat", m))
                b = bank_of("kvlat", m)
                f(lat_sq[:, 512 * (m + 1):512 * (m + 2)], b, ACT.Square).then_inc(own.up("lat_sq"), 1)
                f(KVL[:, m, :], b).then_inc(own.frees("kvlat", m), 1)
            eng.wait_ge(product_ready, made("krope"))
            b = bank_of("krope")
            f(kr_raw[0:ROPE, :], b[0:ROPE, :]).then_inc(own.frees("krope"), 1)
            eng.wait_ge(product_ready, made("qssq"))
            b = bank_of("qssq")
            f(rstd[:, 0:T], b[:, 0:T], ACT.Sqrt, scale=1.0 / 256, bias=eps_rms).then_inc(own.frees("qssq"), 1)
            eng.wait_ge(product_ready, made("kvssq"))
            b = bank_of("kvssq")
            f(t4[:, 0, :], b, ACT.Sqrt, scale=1.0 / 256, bias=eps_rms).then_inc(own.frees("kvssq"), 1)
            eng.dma_start(region(6), tables_d[:, 5120:7168]).then_inc(s.sem("pool_table"), 16)
            for j in range(4):
                eng.wait_ge(product_ready, made("qh", j))
                b = bank_of("qh", j)
                f(QM[0:96, 2 * j:2 * j + 2, :], halves(b)[0:96]).then_inc(own.frees("qh", j), 1)
            for h in range(MH):
                eng.wait_ge(product_ready, made("knope", h))
                b = bank_of("knope", h)
                f(KM[0:NOPE, h, :], b[0:NOPE, :]).then_inc(own.frees("knope", h), 1)
            eng.wait_ge(s.sem("kr_roped"), 1)
            for h in range(MH):
                f(KM[NOPE:NOPE + ROPE, h, :], kr_raw[0:ROPE, :]).then_inc(own.up("k_filled"), 1)
            eng.wait_ge(s.sem("q_roped"), 4)
            for j in range(2):
                eng.wait_ge(product_ready, made("poold", j))
                b = bank_of("poold", j)
                f(t4[:, j, :], b).then_inc(own.frees("poold", j), 1)
            for j in range(2):
                eng.wait_ge(product_ready, made("poolo", j))
                b = bank_of("poolo", j)
                for i in range(2):
                    ins = f(MIXM[:, 2 * j + i, :], b[:, i * T:(i + 1) * T], scale=vec("pool_scale", 2 * j + i))
                ins.then_inc(own.frees("poolo", j), 1)
            for name, u in attention_order("mla", 2 * MH):
                eng.wait_ge(product_ready, made(name, u))
                b = bank_of(name, u)
                if name == "mla_scores":
                    eng.wait_ge(s.sem("mla_shifted"), u + 1)
                    f(t4[:, u % 4, :], b, ACT.Exp, scale=96 ** -0.5, bias=mstat[:, u, 0:1],
                           accum_out=mstat[:, u, 1:2]).then_inc(own.frees(name, u), 1)
                elif name == "mla_turn":
                    f(mla_pt[:, u % 2, :], b).then_inc(own.frees(name, u), 1)
                else:
                    h, a = u // 2, u % 2
                    rows = slice(64 * (h % 2), 64 * (h % 2) + 64)
                    f(MIXM[rows, 4 + h // 2, a * P:(a + 1) * P], b[0:VH, 0:P]).then_inc(own.frees(name, u), 1)
            layer_norm(0, "mixout", 2, 16)
            eng.dma_start(R[:, :], tables_d[:, 0:3072]).then_inc(s.sem("dft_tables"), 16)
            modulate(H, X, 2, scale_a, modv[:, 2, 24:32])
            feed_forward(2)
            eng.wait_ge(product_ready, made("down2", 3))
            eng.dma_start(region(4), tables_d[:, 3072:5120]).then_inc(s.sem("decay_loaded"), 16)
            layer_norm(1, "down2", 2, 40)
            modulate(H, X, 3, scale_a, modv[:, 3, 0:8])
            for j in range(3):
                eng.wait_ge(s.sem("sin_arg"), j + 1)
                f(sines[:, j, :], TMP[0:64, 1024:1280], ACT.Sin).then_inc(own.up("sine"), 1)
            for j in range(4):
                for n in ("hx1", "hv", "hx0"):
                    stage_in(n, j)
            eng.wait_ge(*drained("filt", 7))
            for j in range(4):
                eng.wait_ge(product_ready, made("wturn", j))
                b = bank_of("wturn", j)
                for a in range(2):
                    ins = f(WTOK[:, a, 256 * j:256 * (j + 1)].rearrange("p (m c) -> p m c", c=P),
                            b.rearrange("p (m a c) -> p m a c", a=2, c=P)[:, :, a, :])
                ins.then_inc(own.frees("wturn", j), 1)
            for half in range(2):
                for n in range(4):
                    eng.wait_ge(product_ready, made("vspec", 4 * half + n))
                    b = bank_of("vspec", 4 * half + n)
                    f(VS[:, n, :], b).then_inc(own.frees("vspec", 4 * half + n), 1)
            layer_norm(2, "hyout", 3, 16)
            modulate(H, X, 4, scale_a, modv[:, 3, 24:32])
            eng.wait_ge(s.sem("top2"), 1)
            f(small[:, 264:266], small[:, 264:266], ACT.Exp).then_inc(own.up("top2_exp"), 1)
            for j in range(4):
                eng.wait_ge(product_ready, made("tokens", j))
                b = bank_of("tokens", j)
                f(TOK[:, :, 256 * j:256 * (j + 1)].rearrange("p a (m c) -> p m a c", c=P),
                  b.rearrange("p (m a c) -> p m a c", a=2, c=P)).then_inc(own.frees("tokens", j), 1)
            eng.wait_ge(s.sem("items_ready"), 1)
            n_items = eng.value_load(items[0:1, 0:1], min_val=EXPERTS, max_val=EXPERTS + EXTRA)
            for h in range(2):
                eng.wait_ge(s.sem("moe_gathered"), h + 1)
                f(XG[:, 4 * h:4 * h + 4, :], s.psum[:, 6 + h, :].rearrange("p (k t) -> p k t", t=P)).then_inc(s.sem("moe_xg"), 1)
            with eng.Fori(0, n_items) as e:
                for q in range(FEJ + 1):
                    if q < FEJ:
                        eng.wait_ge(s.sem("moe_gu"), FEJ * e + q + 1)
                        f(moe_s[:, q % 2, :], s.psum[:, 2 * (q % 2), :], ACT.Silu).then_inc(s.sem("moe_silu"), 1)
                    if q == 0:
                        eng.wait_ge(s.sem("sel_turned"), e + 1)
                        f(sel_t, s.psum[:, 6, 0:T]).then_inc(s.sem("sel_t_ready"), 1)
                    if q >= 1:
                        eng.wait_ge(s.sem("moe_t"), FEJ * e + q)
                        f(moe_ht[:, (q - 1) % 2, :], s.psum[:, 2 * ((q - 1) % 2), :]).then_inc(s.sem("moe_turned"), 1)
                c = MOE_BASE + 3 * FEJ - 1
                eng.wait_ge(s.sem(f"used{c % RING}"), 3 * e + (c // RING + 1))
                for n in range(2):
                    f(YG[:, n * 512:(n + 1) * 512], s.psum[:, 4 + n, :]).then_inc(s.sem("moe_y"), 1)
                for h in range(2):
                    eng.wait_ge(s.sem("moe_gathered"), 2 * e + 3 + h)
                    f(XG[:, 4 * h:4 * h + 4, :], s.psum[:, 6 + h, :].rearrange("p (k t) -> p k t", t=P)).then_inc(s.sem("moe_xg"), 1)
            layer_norm(3, "moeturn", 3, 40)

        @block.vector
        def _(eng):
            own = Count(s, bank_free)

            def tt(out, a, b, op=ALU.mult):
                return eng.tensor_tensor(out, a, b, op)

            def ts(out, a, s1, s2=None, op0=ALU.mult, op1=ALU.bypass):
                return eng.tensor_scalar(out, a, s1, s2, op0, op1)

            def stt(out, a, scalar, b, op0=ALU.mult, op1=ALU.add):
                return eng.scalar_tensor_tensor(out=out, in0=a, scalar=scalar, in1=b, op0=op0, op1=op1)

            def over(ap, n):
                return ap.unsqueeze(1).broadcast_to((ap.shape[0], n, ap.shape[1]))

            def along(ap, n):
                return ap.unsqueeze(2).broadcast_to((ap.shape[0], ap.shape[1], n))

            mods = [0, 0]

            def mod_read():
                d = mods[1]
                mods[1] += 1
                eng.wait_ge(product_ready, made("mod", d))
                b = bank_of("mod", d)
                layer, at = d // 12, 4 * (d % 12)
                ins = tt(modv[:, layer, at:at + 4], b[:, 0:4], vec("mod_b", 48 * layer + at, 4), ALU.add)
                if 24 <= d < 28:
                    ins.then_inc(own.up("dve_step"), 1)
                    ins = tt(modx[:, at:at + 4], b[:, 4:8], vec("mod_b", 96 + at, 4), ALU.add)
                ins.then_inc(own.frees("mod", d), 1)
                eng.wait_ge(own.sem, own.value)
                ts(small[:, 63:64], small[:, 0:1], 1.0).then_inc(own.up("mod_done"), 1)

            def mod_chunk():
                d = mods[0]
                mods[0] += 1
                while mods[1] <= d - 2:
                    mod_read()
                c = D_CHUNKS[d]
                eng.wait_ge(s.sem(f"landed{c % RING}"), 16 * (c // RING + 1))
                w = ring[:, c % RING, :]
                acc = mod_acc[:, d % 2, :]
                cv = 0 if d < 24 else 16
                accs = [(acc, cv)]
                if 24 <= d < 28:
                    accs.insert(0, (R[:, 512 * (d % 2):512 * (d % 2) + 512], 8))
                for n, (dst, at) in enumerate(accs):
                    for k in range(KT):
                        ck = c_act[:, at + k:at + k + 1]
                        wk = w[:, k * 512:(k + 1) * 512]
                        ins = ts(dst, wk, ck) if k == 0 else stt(dst, wk, ck, dst)
                        if k < KT - 1:
                            ins.then_inc(own.up("dve_step"), 1)
                            eng.wait_ge(own.sem, own.value)
                    if n < len(accs) - 1:
                        ins.then_inc(own.up("ctx_acc"), 1)
                ins.then_inc(s.sem(f"used{c % RING}"), 1)
                own.sem, own.value = s.sem(f"used{c % RING}"), c // RING + 1

            def flush_mods():
                while mods[1] < mods[0]:
                    mod_read()

            def pre_norm(n, layer, half, gain):
                if n:
                    eng.wait_ge(s.sem("h_ready"), 8 * n)
                stt(scale_a, modv[:, layer, 24 * half + 8:24 * half + 16], 1.0, gain, ALU.add, ALU.mult).then_inc(own.up("dve_step"), 1)
                eng.wait_ge(own.sem, own.value)
                eng.wait_ge(*drained("ssq", 2 * n))
                eng.reciprocal(rstd[:, 0:T], rstd[:, 0:T]).then_inc(own.up("dve_step"), 1)
                eng.wait_ge(own.sem, own.value)
                for k in range(KT):
                    tt(H[:, k, :], X[:, k, :], rstd[:, 0:T]).then_inc(own.up("normed"), 1)

            def post_norm(n, name, layer, half, gain):
                eng.wait_ge(own.sem, own.value)
                stt(shift_c, modv[:, layer, 24 * half + 16:24 * half + 24], 1.0, gain, ALU.add, ALU.mult).then_inc(own.up("dve_step"), 1)
                eng.wait_ge(own.sem, own.value)
                eng.wait_ge(*drained("ssq", n))
                eng.reciprocal(rstd[:, 0:T], rstd[:, 0:T]).then_inc(own.up("dve_step"), 1)
                eng.wait_ge(own.sem, own.value)
                for j in range(4):
                    eng.wait_ge(*drained(name, j))
                    tt(Y[:, 2 * j:2 * j + 2, :], Y[:, 2 * j:2 * j + 2, :], over(rstd[:, 0:T], 2)).then_inc(own.up("dve_step"), 1)
                eng.wait_ge(own.sem, own.value)
                for k in range(KT):
                    ins = stt(X[:, k, :], Y[:, k, :], shift_c[:, k:k + 1], X[:, k, :])
                ins.then_inc(own.up("x1_ready"), 1)
                eng.wait_ge(own.sem, own.value)

            def conv(name, j, dst, taps, first, w_at, bias_at, stride):
                n = staged(name, j)
                for tap in range(taps):
                    for i in range(2):
                        k = 2 * j + i
                        x = stage[:, n % 2, i, first + tap:first + tap + T]
                        w = vec(w_at[0], w_at[1] + tap * stride + k)
                        if tap == 0:
                            ins = ts(dst[i], x, w, vec(bias_at[0], bias_at[1] + k), ALU.mult, ALU.add)
                        else:
                            ins = stt(dst[i], x, w, dst[i])
                        if i and tap == taps - 1:
                            ins.then_inc(own.up("conv_done"), 1)
                        else:
                            ins.then_inc(own.up("dve_step"), 1)
                    eng.wait_ge(own.sem, own.value)

            def two(ap):
                return [ap[:, 0:T], ap[:, T:2 * T]]

            def feed_forward(tag, n_mods):
                for j in range(FT // 2):
                    if tag < 2:
                        eng.wait_ge(*drained(f"gate{tag}", j))
                        conv(f"gate{tag}", j, two(t4[:, j % 2, :]), 3, 1, ("ffn_conv_w", tag * 3 * FT),
                             ("ffn_conv_b", tag * FT), FT)
                        eng.wait_ge(s.sem("silu"), 11 * tag + j + 1)
                    else:
                        eng.wait_ge(*drained(f"gate{tag}", j))
                    eng.wait_ge(product_ready, made(f"up{tag}", j))
                    b = bank_of(f"up{tag}", j)
                    tt(HID[:, 2 * j:2 * j + 2, :], feat(t4[:, 2 + j % 2, :]), feat(b)).then_inc(own.frees(f"up{tag}", j), 1)
                    if j < n_mods:
                        mod_chunk()
                    elif j == n_mods + 1:
                        flush_mods()
                if n_mods == 12:
                    mod_chunk()
                flush_mods()

            def layer_norm(n):
                for j in range(4):
                    eng.wait_ge(*drained(LN_OF[n], j))
                    xs = X[:, 2 * j:2 * j + 2, :]
                    stt(xs, xs, ALPHA, Y[:, 2 * j:2 * j + 2, :]).then_inc(own.up("z_ready"), 1)
                eng.wait_ge(product_ready, made("mean", n))
                b = bank_of("mean", n)
                mean = t4[:, 0, 0:T]
                ts(mean, b[:, 0:T], 1.0 / D).then_inc(own.frees("mean", n), 1)
                eng.wait_ge(own.sem, own.value)
                for j in range(4):
                    xs = X[:, 2 * j:2 * j + 2, :]
                    tt(xs, xs, over(mean, 2), ALU.subtract).then_inc(own.up("centred"), 1)
                eng.wait_ge(*drained("ssq", 8 + n))
                eng.reciprocal(rstd[:, 0:T], rstd[:, 0:T]).then_inc(own.up("dve_step"), 1)
                eng.wait_ge(own.sem, own.value)
                for j in range(4):
                    xs = X[:, 2 * j:2 * j + 2, :]
                    tt(xs, xs, over(rstd[:, 0:T], 2)).then_inc(own.up("ln_scaled"), 1)

            LN_OF = ["mixout", "down2", "hyout", "moeturn"]

            def coef(n_h, layer, half):
                eng.wait_ge(s.sem("h_ready"), n_h)
                ts(scale_a, modv[:, layer, 24 * half + 8:24 * half + 16], 1.0, None, ALU.add).then_inc(own.up("coef"), 1)

            eng.memset(stage[:, :, :, :], 0.0).then_inc(own.up("dve_step"), 1)
            eng.memset(small[:, 0:1], EPS_RMS).then_inc(own.up("dve_step"), 1)
            eng.memset(small[:, 1:2], EPS_LN).then_inc(own.up("dve_step"), 1)
            eng.wait_ge(own.sem, own.value)
            eng.memset(small[:, 63:64], 0.0).then_inc(own.up("cleared"), 1)
            eng.wait_ge(s.sem("consts_loaded"), 48)
            lam = vec("lru_lam", 0, 8)
            ts(lru_c, lam, -1.0).then_inc(own.up("dve_step"), 1)
            eng.wait_ge(own.sem, own.value)
            tt(lru_c, lru_c, lam, ALU.max).then_inc(own.up("lam_abs"), 1)
            for _ in range(4):
                if mods[0] == 0:
                    eng.wait_ge(s.sem("c_act"), 1)
                mod_chunk()
            flush_mods()
            eng.wait_ge(s.sem("lam_exp"), 1)
            z, w, w2, acc = lru_cn, hyp[:, 0:8], hyp[:, 8:16], hyp[:, 16:24]
            ts(w, z, 2.0, None, ALU.add).then_inc(own.up("dve_step"), 1)
            eng.wait_ge(own.sem, own.value)
            eng.reciprocal(w, w).then_inc(own.up("dve_step"), 1)
            eng.wait_ge(own.sem, own.value)
            tt(w, w, z).then_inc(own.up("dve_step"), 1)
            eng.wait_ge(own.sem, own.value)
            tt(w2, w, w).then_inc(own.up("dve_step"), 1)
            eng.wait_ge(own.sem, own.value)
            ts(acc, w2, 1.0 / 19, 1.0 / 17, ALU.mult, ALU.add).then_inc(own.up("dve_step"), 1)
            eng.wait_ge(own.sem, own.value)
            for n in range(15, 0, -2):
                tt(acc, acc, w2).then_inc(own.up("dve_step"), 1)
                eng.wait_ge(own.sem, own.value)
                ts(acc, acc, 1.0 / n, None, ALU.add).then_inc(own.up("dve_step"), 1)
                eng.wait_ge(own.sem, own.value)
            stt(acc, acc, 2.0, w, ALU.mult, ALU.mult).then_inc(own.up("dve_step"), 1)
            eng.wait_ge(own.sem, own.value)
            ts(w, lam, -1.0, 0.0, ALU.mult, ALU.max).then_inc(own.up("dve_step"), 1)
            eng.wait_ge(own.sem, own.value)
            tt(acc, acc, w, ALU.add).then_inc(own.up("dve_step"), 1)
            eng.wait_ge(own.sem, own.value)
            ts(lru_c, acc, -8.0).then_inc(own.up("dve_step"), 1)
            eng.wait_ge(own.sem, own.value)
            ts(lru_cn, acc, 8.0).then_inc(own.up("lru_coef"), 1)
            eng.wait_ge(own.sem, own.value)
            pre_norm(0, 0, 0, vec("g_mix_pre", 0, 8))
            for j in range(4):
                eng.wait_ge(*drained("xr", j))
                conv("xr", j, [XC[:, 2 * j, :], XC[:, 2 * j + 1, :]], 4, 0, ("ab_conv_w", 0), ("ab_conv_b", 0), 8)
            for _ in range(4):
                mod_chunk()
            lru_r, lru_i, lru_a, lru_x = feat(region(5)), feat(region(6)), feat(region(4)), feat(TMP[:, :])
            for j in range(4):
                p2 = slice(2 * j, 2 * j + 2)
                eng.wait_ge(s.sem("lru_t"), 2 * j + 2)
                ts(lru_x[:, p2, :], lru_r[:, p2, :], 1.0, None, ALU.add).then_inc(own.up("dve_step"), 1)
                eng.wait_ge(own.sem, own.value)
                eng.reciprocal(lru_x[:, p2, :], lru_x[:, p2, :]).then_inc(own.up("dve_step"), 1)
                eng.wait_ge(own.sem, own.value)
                tt(lru_r[:, p2, :], lru_r[:, p2, :], lru_x[:, p2, :]).then_inc(own.up("lru_w"), 1)
            for j in range(4):
                p2 = slice(2 * j, 2 * j + 2)
                eng.wait_ge(*drained("i", j))
                tt(lru_i[:, p2, :], lru_i[:, p2, :], XC[:, p2, :]).then_inc(own.up("dve_step"), 1)
                eng.wait_ge(own.sem, own.value)
                eng.wait_ge(s.sem("lru_s"), j + 1)
                tt(lru_i[:, p2, :], lru_i[:, p2, :], lru_r[:, p2, :]).then_inc(own.up("dve_step"), 1)
                eng.wait_ge(own.sem, own.value)
                for k in (2 * j, 2 * j + 1):
                    eng.tensor_tensor_scan(lru_x[:, k, :], lru_a[:, k, :], lru_i[:, k, :], 0.0,
                                               ALU.mult, ALU.add).then_inc(own.up("dve_step"), 1)
                eng.wait_ge(own.sem, own.value)
                eng.wait_ge(*drained("gr", j))
                tt(MIX[:, p2, :], MIX[:, p2, :], lru_x[:, p2, :]).then_inc(own.up("rnn_mixed"), 1)
            eng.wait_ge(own.sem, own.value)
            for _ in range(4):
                mod_chunk()
            flush_mods()
            for j in range(6):
                eng.wait_ge(product_ready, made("rope", j))
                b = feat(bank_of("rope", j))
                n = 2 * j if j < 4 else 2 * (j - 4)
                src = (QRAW if j < 4 else KSKW)[:, n:n + 2, :]
                dst = (QROT if j < 4 else KSKW)[:, n:n + 2, :]
                tmp = feat(t4[:, 0, :])
                tt(tmp, b, over(const("rope_sin"), 2)).then_inc(own.frees("rope", j), 1)
                eng.wait_ge(own.sem, own.value)
                tt(dst, src, over(const("rope_cos"), 2)).then_inc(own.up("dve_step"), 1)
                eng.wait_ge(own.sem, own.value)
                tt(dst, dst, tmp, ALU.add).then_inc(own.up("roped"), 1)
                eng.wait_ge(own.sem, own.value)
            for i in range(2):
                eng.wait_ge(product_ready, made("cmp_h", i))
                b = bank_of("cmp_h", i)
                eng.tensor_copy(cmp_bias[:, i:i + 1], b[:, 64:65]).then_inc(own.up("cmp_bias"), 1)
            for a in range(2):
                neg = CCOL["cmp_neg"][0] + a * NCMP
                one = CCOL["cmp_one"][0] + a * NCMP
                heads = cx[:, a].rearrange("p (gp half r) n -> p gp half r n", half=2, r=REP)
                for half in range(2):
                    eng.wait_ge(product_ready, made("sc", 2 * a + half))
                    b = bank_of("sc", 2 * a + half)
                    for gp in range(2):
                        ins = tt(heads[:, gp, half], b[:, 60 * gp:60 * gp + 60].rearrange("p (r n) -> p r n", n=NCMP),
                                 over(consts[:, neg:neg + NCMP], REP), ALU.add)
                    ins.then_inc(own.frees("sc", 2 * a + half), 1)
                eng.wait_ge(own.sem, own.value)
                eng.tensor_reduce(cstat[:, a, 0], cx[:, a], AX.X, ALU.max).then_inc(own.up("dve_step"), 1)
                eng.wait_ge(own.sem, own.value)
                tt(cx[:, a], cx[:, a], along(cstat[:, a, 0], NCMP), ALU.subtract).then_inc(own.up("cmp_shifted"), 1)
                eng.wait_ge(s.sem("cmp_exp"), a + 1)
                eng.tensor_reduce(cstat[:, a, 1], cx[:, a], AX.X, ALU.add).then_inc(own.up("dve_step"), 1)
                eng.wait_ge(own.sem, own.value)
                eng.reciprocal(cstat[:, a, 1], cstat[:, a, 1]).then_inc(own.up("dve_step"), 1)
                eng.wait_ge(own.sem, own.value)
                eng.wait_ge(*drained("gates"))
                tt(cstat[:, a, 1], cstat[:, a, 1], gates[:, a, :, 0]).then_inc(own.up("dve_step"), 1)
                eng.wait_ge(own.sem, own.value)
                tt(cx[:, a], cx[:, a], over(consts[:, one:one + NCMP], HEADS)).then_inc(own.up("dve_step"), 1)
                eng.wait_ge(own.sem, own.value)
                tt(cx[:, a], cx[:, a], along(cstat[:, a, 1], NCMP)).then_inc(own.up("cmp_probs"), 1)
            eng.wait_ge(own.sem, own.value)

            def nsa_shift(u):
                a = u % 2
                nk = (a + 1) * P
                eng.wait_ge(product_ready, made("nsa_scores", u))
                b = feat(bank_of("nsa_scores", u))[:, :, 0:nk]
                x = feat(t4[:, u % 4, :])[:, :, 0:nk]
                mask = const("causal")[:, T - nk:T]
                tt(x, b, over(mask, 2), ALU.add).then_inc(own.frees("nsa_scores", u), 1)
                eng.wait_ge(own.sem, own.value)
                eng.tensor_reduce(sstat[:, u, :, 0], x, AX.X, ALU.max, negate=True).then_inc(own.up("dve_step"), 1)
                eng.wait_ge(own.sem, own.value)
                ts(sstat[:, u, :, 0], sstat[:, u, :, 0], HD ** -0.5).then_inc(own.up("shifted"), 1)

            def nsa_scale(u):
                a, hh = u % 2, u // 2
                h = 4 * (2 * (hh // 2 // 4) + hh % 2) + hh // 2 % 4
                nk = (a + 1) * P
                eng.wait_ge(s.sem("exps"), 2 * u + 2)
                eng.reciprocal(sstat[:, u, :, 2], sstat[:, u, :, 1]).then_inc(own.up("dve_step"), 1)
                eng.wait_ge(own.sem, own.value)
                tt(sstat[:, u, :, 2], sstat[:, u, :, 2], gates[:, a, h, 1:3]).then_inc(own.up("dve_step"), 1)
                eng.wait_ge(own.sem, own.value)
                for w in range(2):
                    x = t4[:, u % 4, w * T:w * T + nk]
                    ins = ts(x, x, sstat[:, u, w, 2:3])
                ins.then_inc(own.up("probs"), 1)

            for u in range(2 * HEADS + 1):
                if u < 2 * HEADS:
                    nsa_shift(u)
                if u:
                    nsa_scale(u - 1)
            post_norm(1, "about", 0, 0, vec("g_mix_post", 0, 8))
            pre_norm(1, 0, 1, vec("g_ffn_pre", 0, 8))
            feed_forward(0, 12)
            post_norm(3, "down0", 0, 1, vec("g_ffn_post", 0, 8))
            pre_norm(2, 1, 0, vec("g_mix_pre", 8, 8))
            for j in range(4):
                n = staged("cv", j)
                eng.wait_ge(*drained("cg", j))
                eng.wait_ge(product_ready, made("scv", j))
                b = bank_of("scv", j)
                tt(stage[:, n % 2, :, 3:259], feat(t4[:, j % 2, :]), feat(b)).then_inc(own.frees("scv", j), 1)
                eng.wait_ge(own.sem, own.value)
                conv("cv", j, two(t4[:, 2 + j % 2, :]), 3, 1, ("sc_conv_w", 0), ("sc_conv_b", 0), 8)
                eng.wait_ge(product_ready, made("bg", j))
                b = bank_of("bg", j)
                tt(MIX[:, 2 * j:2 * j + 2, :], feat(t4[:, 2 + j % 2, :]), feat(b)).then_inc(own.frees("bg", j), 1)
                mod_chunk()
                mod_chunk()
            flush_mods()
            post_norm(5, "scout", 1, 0, vec("g_mix_post", 8, 8))
            pre_norm(3, 1, 1, vec("g_ffn_pre", 8, 8))
            feed_forward(1, 12)
            post_norm(7, "down1", 1, 1, vec("g_ffn_post", 8, 8))
            eng.wait_ge(s.sem("h_ready"), 32)
            ts(scale_x, modx[:, 8:16], 1.0, None, ALU.add).then_inc(own.up("dve_step"), 1)
            eng.wait_ge(own.sem, own.value)
            coef(32, 2, 0)
            eng.wait_ge(*drained("qssq"))
            eng.reciprocal(rstd[:, 0:T], rstd[:, 0:T]).then_inc(own.up("dve_step"), 1)
            eng.wait_ge(own.sem, own.value)
            for k in range(2):
                stt(QL[:, k, :], QL[:, k, :], vec("q_norm", k), rstd[:, 0:T], ALU.mult, ALU.mult).then_inc(own.up("q_normed" if k else "dve_step"), 1)
            eng.wait_ge(*drained("kvssq"))
            eng.reciprocal(t4[:, 0, :], t4[:, 0, :]).then_inc(own.up("dve_step"), 1)
            eng.wait_ge(own.sem, own.value)
            for k in range(2):
                stt(KVL[:, k, :], KVL[:, k, :], vec("kv_norm", k), t4[:, 0, :], ALU.mult, ALU.mult).then_inc(own.up("kv_normed" if k else "dve_step"), 1)
            eng.wait_ge(product_ready, made("krot"))
            b = bank_of("krot")
            kr = kr_raw[0:ROPE, 0:T]
            tt(kr_tmp[0:ROPE, 0:T], b[0:ROPE, 0:T], const("kr_sin", ROPE)).then_inc(own.frees("krot"), 1)
            eng.wait_ge(own.sem, own.value)
            tt(kr, kr, const("kr_cos", ROPE)).then_inc(own.up("dve_step"), 1)
            eng.wait_ge(own.sem, own.value)
            tt(kr, kr, kr_tmp[0:ROPE, 0:T], ALU.add).then_inc(own.up("kr_roped"), 1)
            for kt in range(4):
                eng.wait_ge(product_ready, made("vm", kt))
                b = bank_of("vm", kt)
                eng.tensor_copy(VM[:, kt, :], b).then_inc(own.frees("vm", kt), 1)
            for j in range(4):
                eng.wait_ge(product_ready, made("qrot", j))
                b = feat(bank_of("qrot", j))[0:96]
                qs = QM[0:96, 2 * j:2 * j + 2, :]
                tmp = feat(t4[:, 1, :])[0:96]
                tt(tmp, b, over(const("mla_sin", 96), 2)).then_inc(own.frees("qrot", j), 1)
                eng.wait_ge(own.sem, own.value)
                tt(qs, qs, over(const("mla_cos", 96), 2)).then_inc(own.up("dve_step"), 1)
                eng.wait_ge(own.sem, own.value)
                tt(qs, qs, tmp, ALU.add).then_inc(own.up("q_roped"), 1)
                eng.wait_ge(own.sem, own.value)
            for u in range(2 * MH + 1):
                if u < 2 * MH:
                    eng.wait_ge(product_ready, made("mla_scores", u))
                    b = bank_of("mla_scores", u)
                    eng.tensor_reduce(mstat[:, u, 0:1], b, AX.X, ALU.max, negate=True).then_inc(own.up("dve_step"), 1)
                    eng.wait_ge(own.sem, own.value)
                    ts(mstat[:, u, 0:1], mstat[:, u, 0:1], 96 ** -0.5).then_inc(own.up("mla_shifted"), 1)
                if u:
                    v = u - 1
                    eng.wait_ge(*drained("mla_scores", v))
                    eng.reciprocal(mstat[:, v, 2:3], mstat[:, v, 1:2]).then_inc(own.up("dve_step"), 1)
                    eng.wait_ge(own.sem, own.value)
                    ts(t4[:, v % 4, :], t4[:, v % 4, :], mstat[:, v, 2:3]).then_inc(own.up("mla_probs"), 1)
            layer_norm(0)
            coef(48, 2, 1)
            feed_forward(2, 4)
            layer_norm(1)
            coef(56, 3, 0)
            arg, turns = TMP[0:64, 1024:1280], TMP[0:64, 1280:1536]
            c1 = 6.28125
            c2 = 0.00193500518798828125
            c3 = 2 * math.pi - c1 - c2
            magic = 1.5 * 2.0 ** 23
            pi_lo = 3.1415925
            for j in range(3):
                eng.wait_ge(product_ready, made("sin", j))
                b = bank_of("sin", j)
                if j:
                    eng.wait_ge(s.sem("sine"), j)
                ts(arg, b[0:64, 0:T], vec("hy_fb", j, 1, 64), vec("hy_freq", 0, 1, 64), ALU.add, ALU.mult).then_inc(own.frees("sin", j), 1)
                eng.wait_ge(own.sem, own.value)
                ts(turns, arg, 1.0 / (2 * math.pi)).then_inc(own.up("dve_step"), 1)
                eng.wait_ge(own.sem, own.value)
                ts(turns, turns, magic, None, ALU.add).then_inc(own.up("dve_step"), 1)
                eng.wait_ge(own.sem, own.value)
                ts(turns, turns, -magic, None, ALU.add).then_inc(own.up("dve_step"), 1)
                eng.wait_ge(own.sem, own.value)
                for c in (c1, c2, c3):
                    stt(arg, turns, -c, arg).then_inc(own.up("dve_step"), 1)
                    eng.wait_ge(own.sem, own.value)
                ts(arg, arg, pi_lo, -pi_lo, ALU.min, ALU.max).then_inc(own.up("sin_arg"), 1)
            eng.wait_ge(s.sem("decay_loaded"), 16)
            for j in range(8):
                a, n = j // 4, j % 4
                eng.wait_ge(product_ready, made("filt", j))
                b = bank_of("filt", j)
                tt(HF[:, a, n * 512:(n + 1) * 512], b, DECAY[:, a, (n % 2) * 512:(n % 2 + 1) * 512]).then_inc(own.frees("filt", j), 1)
            for j in range(4):
                for name, dst, at in (("hx1", two(t4[:, 0, :]), 8), ("hv", two(t4[:, 1, :]), 16),
                                      ("hx0", [X0[:, 2 * j, :], X0[:, 2 * j + 1, :]], 0)):
                    eng.wait_ge(*drained(name, j))
                    conv(name, j, dst, 3, 2, ("hy_conv_w", at), ("hy_conv_b", at), 24)
                tt(WF[:, 2 * j:2 * j + 2, :], feat(t4[:, 0, :]), feat(t4[:, 1, :])).then_inc(own.up("w_ready"), 1)
                eng.wait_ge(own.sem, own.value)
            for half in range(2):
                for i in range(2):
                    eng.wait_ge(*drained("vspec", 4 * half + 2 + i))
                    eng.wait_ge(product_ready, made("kre", 2 * half + i))
                    kre = bank_of("kre", 2 * half + i)
                    eng.wait_ge(product_ready, made("kim", 2 * half + i))
                    kim = bank_of("kim", 2 * half + i)
                    tt(t4[:, 0, :], VS[:, i, :], kre).then_inc(own.up("dve_step"), 1)
                    tt(t4[:, 3, :], VS[:, 2 + i, :], kre).then_inc(own.frees("kre", 2 * half + i), 1)
                    tt(t4[:, 1, :], VS[:, 2 + i, :], kim).then_inc(own.up("dve_step"), 1)
                    tt(t4[:, 2, :], VS[:, i, :], kim).then_inc(own.frees("kim", 2 * half + i), 1)
                    eng.wait_ge(own.sem, own.value)
                    tt(VS[:, i, :], t4[:, 0, :], t4[:, 1, :], ALU.subtract).then_inc(own.up("dve_step"), 1)
                    tt(VS[:, 2 + i, :], t4[:, 2, :], t4[:, 3, :], ALU.add).then_inc(own.up("dve_step"), 1)
                    eng.wait_ge(own.sem, own.value)
                    if i == 0:
                        eng.tensor_copy(VS[0:1, 0, :], t4[0:1, 0, :]).then_inc(own.up("dve_step"), 1)
                        eng.tensor_copy(VS[0:1, 2, :], t4[0:1, 1, :]).then_inc(own.up("dve_step"), 1)
                        eng.wait_ge(own.sem, own.value)
                    ts(small[:, 63:64], small[:, 0:1], 1.0).then_inc(own.up("spectrum"), 1)
                for j in range(2):
                    eng.wait_ge(product_ready, made("hconv", 2 * half + j))
                    b = bank_of("hconv", 2 * half + j)
                    for i in range(2):
                        m = 4 * half + 2 * j + i
                        ins = stt(t4[:, 0, i * T:(i + 1) * T], WF[:, m, :], vec("hy_skip", m), b[:, i * T:(i + 1) * T])
                    ins.then_inc(own.frees("hconv", 2 * half + j), 1)
                    eng.wait_ge(own.sem, own.value)
                    m = 4 * half + 2 * j
                    tt(WF[:, m:m + 2, :], feat(t4[:, 0, :]), X0[:, m:m + 2, :]).then_inc(own.up("hy_mixed"), 1)
                    eng.wait_ge(own.sem, own.value)
            layer_norm(2)
            coef(64, 3, 1)
            eng.wait_ge(product_ready, made("logits"))
            b = bank_of("logits")
            logit, top, ids = hyp[:, 16:32], hyp[:, 32:48], small[:, 272:288]
            eng.tensor_copy(logit, b[:, 0:16]).then_inc(own.frees("logits"), 1)
            eng.wait_ge(own.sem, own.value)
            gap, den = small[:, 264:266], small[:, 266:268]
            for a in range(2):
                e8 = slice(8 * a, 8 * a + 8)
                eng.max(top[:, e8], logit[:, e8]).then_inc(own.up("dve_step"), 1)
                eng.wait_ge(own.sem, own.value)
                eng.max_index(idx[:, a, :], top[:, e8], logit[:, e8]).then_inc(own.up("dve_step"), 1)
                eng.wait_ge(own.sem, own.value)
                eng.tensor_copy(ids[:, e8], idx[:, a, :]).then_inc(own.up("dve_step"), 1)
                eng.wait_ge(own.sem, own.value)
                tt(gap[:, a:a + 1], top[:, 8 * a + 1:8 * a + 2], top[:, 8 * a:8 * a + 1], ALU.subtract).then_inc(own.up("dve_step"), 1)
                eng.wait_ge(own.sem, own.value)
            ts(small[:, 63:64], small[:, 0:1], 1.0).then_inc(own.up("top2"), 1)
            iota = vec("iota", 0, 8)
            for a in range(2):
                ts(chosen[:, a, :], iota, ids[:, 8 * a:8 * a + 1], None, ALU.is_equal).then_inc(own.up("dve_step"), 1)
                eng.wait_ge(own.sem, own.value)
                stt(chosen[:, a, :], iota, ids[:, 8 * a + 1:8 * a + 2], chosen[:, a, :], ALU.is_equal, ALU.add).then_inc(own.up("chosen_made"), 1)
                eng.wait_ge(own.sem, own.value)
            ts(small[:, 63:64], small[:, 0:1], 1.0).then_inc(own.up("chosen_ready"), 1)
            eng.memset(ACC, 0.0).then_inc(own.up("dve_step"), 1)
            eng.memset(table, 0.0).then_inc(own.up("dve_step"), 1)
            eng.wait_ge(s.sem("top2_exp"), 1)
            ts(den, gap, 1.0, None, ALU.add).then_inc(own.up("dve_step"), 1)
            eng.wait_ge(own.sem, own.value)
            eng.reciprocal(den, den).then_inc(own.up("dve_step"), 1)
            eng.wait_ge(own.sem, own.value)
            tt(gap, gap, den).then_inc(own.up("dve_step"), 1)
            eng.wait_ge(own.sem, own.value)
            for a in range(2):
                ts(COMB[:, a, :], iota, ids[:, 8 * a:8 * a + 1], den[:, a:a + 1], ALU.is_equal, ALU.mult).then_inc(own.up("dve_step"), 1)
                ts(top[:, 8 * a:8 * a + 8], iota, ids[:, 8 * a + 1:8 * a + 2], gap[:, a:a + 1], ALU.is_equal, ALU.mult).then_inc(own.up("dve_step"), 1)
                eng.wait_ge(own.sem, own.value)
                tt(by_expert[:, 2 + a, :], COMB[:, a, :], top[:, 8 * a:8 * a + 8], ALU.add).then_inc(own.up("dve_step"), 1)
            eng.tensor_copy(by_expert[:, 4, :], iota).then_inc(own.up("dve_step"), 1)
            eng.wait_ge(product_ready, made("places"))
            b = bank_of("places")
            places = by_expert[:, 0:2, :]
            stt(places, b[:, 0:16].rearrange("p (a e) -> p a e", a=2), 1.0, chosen, ALU.add, ALU.mult).then_inc(own.up("dve_step"), 1)
            ts(over_full, b[:, 16:24], float(P), None, ALU.is_gt).then_inc(own.frees("places"), 1)
            eng.wait_ge(own.sem, own.value)
            ts(places, places, -1.0, None, ALU.add).then_inc(own.up("dve_step"), 1)
            eng.memset(rank[:, 0:1], 0.0).then_inc(own.up("dve_step"), 1)
            eng.wait_ge(own.sem, own.value)
            for e in range(EXPERTS):
                tt(rank[:, e + 1:e + 2], rank[:, e:e + 1], over_full[:, e:e + 1], ALU.add).then_inc(own.up("dve_step"), 1)
                eng.wait_ge(own.sem, own.value)
            eng.tensor_copy(table[:, 0:EXPERTS, :], by_expert.rearrange("p c e -> p e c")).then_inc(own.up("dve_step"), 1)
            for x in range(EXTRA):
                stt(hot, rank[:, 0:EXPERTS], float(x), over_full, ALU.is_equal, ALU.mult).then_inc(own.up("dve_step"), 1)
                eng.wait_ge(own.sem, own.value)
                tt(picked, by_expert, over(hot, 5)).then_inc(own.up("dve_step"), 1)
                eng.wait_ge(own.sem, own.value)
                eng.tensor_reduce(table[:, EXPERTS + x, :], picked, AX.X, ALU.add).then_inc(own.up("dve_step"), 1)
                eng.wait_ge(own.sem, own.value)
            second = table[:, EXPERTS:EXPERTS + EXTRA, 0:2]
            ts(second, second, -float(P), None, ALU.add).then_inc(own.up("dve_step"), 1)
            ts(head[:, 0:1], rank[:, EXPERTS:EXPERTS + 1], float(EXPERTS), None, ALU.add).then_inc(own.up("dve_step"), 1)
            ts(head[:, 1:2], rank[:, EXPERTS:EXPERTS + 1], 1.0).then_inc(own.up("dve_step"), 1)
            ts(head[:, 2:2 + EXTRA], table[:, EXPERTS:EXPERTS + EXTRA, 4], 1.0).then_inc(own.up("dve_step"), 1)
            eng.wait_ge(own.sem, own.value)
            eng.tensor_copy(items[:, :], head).then_inc(own.up("items_ready"), 1)
            for a in range(2):
                ins = ts(sel[:, a, :], const("slots"), table[:, 0, a:a + 1], None, ALU.is_equal)
            ins.then_inc(s.sem("sel_made"), 1)
            ts(small[:, 63:64], small[:, 0:1], 1.0).then_inc(s.sem("moe_acc"), 4)
            eng.wait_ge(s.sem("moe_acc"), 4)
            eng.wait_ge(s.sem("items_ready"), 1)
            n_items = eng.value_load(items[0:1, 0:1], min_val=EXPERTS, max_val=EXPERTS + EXTRA)
            with eng.Fori(0, n_items) as e:
                for q in range(FEJ):
                    eng.wait_ge(s.sem("moe_silu"), FEJ * e + q + 1)
                    tt(moe_h[:, q % 2, :], moe_s[:, q % 2, :], s.psum[:, 2 * (q % 2) + 1, :]).then_inc(s.sem("moe_h"), 1)
                    if q == 0:
                        eng.tensor_copy(place_now, table[:, bass.ds(e + 1, 1), 0:2].rearrange("p a b -> p (a b)")).then_inc(s.sem("place_now"), 1)
                        eng.tensor_copy(comb_now, table[:, bass.ds(e, 1), 2:4].rearrange("p a b -> p (a b)")).then_inc(s.sem("comb_now"), 1)
                        eng.wait_ge(s.sem("place_now"), e + 1)
                        eng.wait_ge(s.sem("sel_turned"), e + 1)
                        for a in range(2):
                            ins = ts(sel[:, a, :], const("slots"), place_now[:, a:a + 1], None, ALU.is_equal)
                        ins.then_inc(s.sem("sel_made"), 1)
                        eng.wait_ge(s.sem("sel_made"), e + 2)
                eng.wait_ge(s.sem("comb_now"), e + 1)
                for a in range(2):
                    for n in range(2):
                        eng.wait_ge(s.sem("moe_out"), 4 * e + 2 * a + n + 1)
                        part = ACC[:, a, n * 512:(n + 1) * 512]
                        stt(part, s.psum[:, 2 * a + n, :], comb_now[:, a:a + 1], part).then_inc(s.sem("moe_acc"), 1)
                eng.wait_ge(s.sem("moe_acc"), 4 * e + 8)
            layer_norm(3)


def kernel(**inputs):
    import concourse.bacc as bacc
    from concourse.bass_utils import run_bass_kernel_spmd

    a = {k: np.asarray(v) for k, v in inputs.items()}
    arrays = host_layout(a)
    nc = bacc.Bacc("TRN2", target_bir_lowering=False, num_devices=1, dynamic_dma_scratch_size=1024)
    aps = [nc.dram_tensor(f"in_{n}", v.shape, mybir.dt.from_np(v.dtype), kind="ExternalInput").ap()
           for n, v in arrays.items()]
    out = nc.dram_tensor("out_t", (P, KT, T), F32, kind="ExternalOutput").ap()
    build(nc, *aps, out)
    r = run_bass_kernel_spmd(nc, [{f"in_{n}": v for n, v in arrays.items()}], core_ids=[0])
    y = r.results[0]["out_t"]
    return np.ascontiguousarray(y.transpose(1, 0, 2).reshape(D, T).T).reshape(1, T, D)
```
